# Optimizing a Trainium2 kernel written in Bass

```python
import jax, jax.numpy as jnp
from jax import lax
import numpy as np
import jax
import jax.numpy as jnp

D_MODEL = 1024
BATCH = 1
SEQ = 256
DEPTH = 2

PLE_DIM = 256
EPS = 1e-6
CHUNK = 64
ROPE_THETA = 10000.0
RET_HEADS = 4
RET_DK = 128
RET_DV = 256
RET_QK = RET_HEADS * RET_DK
RET_V = RET_HEADS * RET_DV
GDN_HEADS = 8
GDN_DK = 128
GDN_DV = 128
GDN_QK = GDN_HEADS * GDN_DK
GDN_V = GDN_HEADS * GDN_DV
GDN_CONV_DIM = 2 * GDN_QK + GDN_V
CONV_WIDTH = 4
D_FF = 2816
N_EXPERTS = 8
TOP_K = 2
D_FF_EXPERT = 1408
N_DENSE = (DEPTH + 1) // 2
N_MOE = DEPTH // 2
OFF_RQ = RET_QK
OFF_RK = OFF_RQ + RET_QK
OFF_RV = OFF_RK + RET_V
OFF_RG = OFF_RV + RET_V
OFF_GQKV = OFF_RG + GDN_CONV_DIM
OFF_GZ = OFF_GQKV + GDN_V
OFF_GA = OFF_GZ + GDN_HEADS
OFF_GB = OFF_GA + GDN_HEADS
OFF_MG_RET = OFF_GB + D_MODEL
D_IN = OFF_MG_RET + D_MODEL
SPLIT_IDX = (OFF_RQ, OFF_RK, OFF_RV, OFF_RG, OFF_GQKV, OFF_GZ, OFF_GA, OFF_GB, OFF_MG_RET)


def rmsnorm(x, g):
    x32 = x.astype(jnp.float32)
    y = x32 * lax.rsqrt(jnp.mean(x32 * x32, axis=-1, keepdims=True) + EPS)
    return (y * g.astype(jnp.float32)).astype(x.dtype)

def l2norm(x):
    return x * lax.rsqrt(jnp.sum(x * x, axis=-1, keepdims=True) + EPS)

def rotary(x, pos):
    half = x.shape[-1] // 2
    inv_freq = ROPE_THETA ** (-jnp.arange(half, dtype=jnp.float32) / half)
    ang = pos[:, None] * inv_freq[None, :]
    cos = jnp.cos(ang)[None, :, None, :]
    sin = jnp.sin(ang)[None, :, None, :]
    x1, x2 = x[..., :half], x[..., half:]
    return jnp.concatenate([x1 * cos - x2 * sin, x2 * cos + x1 * sin], axis=-1)

def causal_conv(x, w):
    width, ch = w.shape
    return lax.conv_general_dilated(
        x, w[:, None, :].astype(x.dtype), window_strides=(1,), padding=[(width - 1, 0)],
        dimension_numbers=("NWC", "WIO", "NWC"), feature_group_count=ch)

def retention(q, k, v):
    B, T, H, dk = q.shape
    dv = v.shape[-1]
    n = T // CHUNK
    log_gamma = jnp.log1p(-jnp.exp2(-5.0 - jnp.arange(H, dtype=jnp.float32)))
    k = k * (dk ** -0.5)
    qc = q.reshape(B, n, CHUNK, H, dk)
    kc = k.reshape(B, n, CHUNK, H, dk)
    vc = v.reshape(B, n, CHUNK, H, dv)
    idx = jnp.arange(CHUNK, dtype=jnp.float32)
    rel = idx[:, None] - idx[None, :]
    causal = rel >= 0
    dmask = jnp.where(causal[None], jnp.exp(jnp.where(causal, rel, 0.0)[None] * log_gamma[:, None, None]), 0.0)
    scores = jnp.einsum("bnihd,bnjhd->bnhij", qc, kc) * dmask
    intra = jnp.einsum("bnhij,bnjhv->bnihv", scores, vc)
    q_dec = qc * jnp.exp((idx + 1.0)[:, None] * log_gamma[None, :])[:, :, None]
    k_dec = kc * jnp.exp((CHUNK - 1.0 - idx)[:, None] * log_gamma[None, :])[:, :, None]
    chunk_decay = jnp.exp(CHUNK * log_gamma)[None, :, None, None]

    def step(R, xs):
        qd, kd, vv = xs
        inter = jnp.einsum("bchd,bhdv->bchv", qd, R)
        R = R * chunk_decay + jnp.einsum("bchd,bchv->bhdv", kd, vv)
        return R, inter

    R0 = jnp.zeros((B, H, dk, dv), jnp.float32)
    _, inter = lax.scan(step, R0, (q_dec.swapaxes(0, 1), k_dec.swapaxes(0, 1), vc.swapaxes(0, 1)))
    out = intra + inter.swapaxes(0, 1)
    return out.reshape(B, T, H, dv)

def gated_delta_rule(q, k, v, g, beta):
    B, T, H, dk = q.shape
    dv = v.shape[-1]
    n = T // CHUNK
    q = q * (dk ** -0.5)

    def to_chunks(t):
        return t.reshape(B, n, CHUNK, H, -1).transpose(0, 3, 1, 2, 4)

    qc, kc, vc = to_chunks(q), to_chunks(k), to_chunks(v)
    gc = jnp.cumsum(g.reshape(B, n, CHUNK, H).transpose(0, 3, 1, 2), axis=-1)
    bc = beta.reshape(B, n, CHUNK, H).transpose(0, 3, 1, 2)[..., None]
    incl = jnp.tril(jnp.ones((CHUNK, CHUNK), bool))
    strict = jnp.tril(jnp.ones((CHUNK, CHUNK), bool), -1)
    diff = gc[..., :, None] - gc[..., None, :]
    decay_incl = jnp.where(incl, jnp.exp(jnp.where(incl, diff, 0.0)), 0.0)
    kb = kc * bc
    a_mat = jnp.einsum("bhnid,bhnjd->bhnij", kb, kc) * jnp.where(strict, decay_incl, 0.0)
    lhs = jnp.eye(CHUNK, dtype=jnp.float32) + a_mat
    u = lax.linalg.triangular_solve(lhs, vc * bc, left_side=True, lower=True, unit_diagonal=True)
    w = lax.linalg.triangular_solve(lhs, kb * jnp.exp(gc)[..., None], left_side=True, lower=True, unit_diagonal=True)
    qk = jnp.einsum("bhnid,bhnjd->bhnij", qc, kc) * decay_incl
    q_dec = qc * jnp.exp(gc)[..., None]
    g_last = gc[..., -1]
    k_dec = kc * jnp.exp(g_last[..., None] - gc)[..., None]

    def step(S, xs):
        qd, qkn, kd, un, wn, gl = xs
        v_new = un - jnp.einsum("bhcd,bhdv->bhcv", wn, S)
        o = jnp.einsum("bhcd,bhdv->bhcv", qd, S) + jnp.einsum("bhij,bhjv->bhiv", qkn, v_new)
        S = S * jnp.exp(gl)[..., None, None] + jnp.einsum("bhcd,bhcv->bhdv", kd, v_new)
        return S, o

    xs = tuple(jnp.moveaxis(t, 2, 0) for t in (q_dec, qk, k_dec, u, w, g_last))
    S0 = jnp.zeros((B, H, dk, dv), jnp.float32)
    _, o = lax.scan(step, S0, xs)
    return jnp.moveaxis(o, 0, 2).transpose(0, 2, 3, 1, 4).reshape(B, T, H, dv)

def mixer_block(h, g_norm, w_in, conv_w, a_log, dt_bias, ret_gn, gdn_gn, w_br_ret, w_br_gdn, w_out, pos):
    B, T, _ = h.shape
    f32 = jnp.float32
    u = rmsnorm(h, g_norm)
    proj = u @ w_in
    rq, rk, rv, rg, gqkv, gz, ga, gb, mg_ret, mg_gdn = jnp.split(proj, SPLIT_IDX, axis=-1)
    q = rotary(rq.reshape(B, T, RET_HEADS, RET_DK).astype(f32), pos)
    k = rotary(rk.reshape(B, T, RET_HEADS, RET_DK).astype(f32), pos)
    v = rv.reshape(B, T, RET_HEADS, RET_DV).astype(f32)
    o = retention(q, k, v)
    mu = jnp.mean(o, axis=-1, keepdims=True)
    var = jnp.mean(jnp.square(o - mu), axis=-1, keepdims=True)
    o = (o - mu) * lax.rsqrt(var + EPS) * ret_gn.astype(f32).reshape(RET_HEADS, RET_DV)
    y_ret = (o.reshape(B, T, RET_V).astype(h.dtype) * jax.nn.silu(rg)) @ w_br_ret
    qkv = jax.nn.silu(causal_conv(gqkv, conv_w))
    gq, gk, gv = jnp.split(qkv, (GDN_QK, 2 * GDN_QK), axis=-1)
    q = l2norm(gq.reshape(B, T, GDN_HEADS, GDN_DK).astype(f32))
    k = l2norm(gk.reshape(B, T, GDN_HEADS, GDN_DK).astype(f32))
    v = gv.reshape(B, T, GDN_HEADS, GDN_DV).astype(f32)
    beta = jax.nn.sigmoid(gb.astype(f32))
    g = -jnp.exp(a_log.astype(f32)) * jax.nn.softplus(ga.astype(f32) + dt_bias.astype(f32))
    o = gated_delta_rule(q, k, v, g, beta)
    o = o * lax.rsqrt(jnp.mean(o * o, axis=-1, keepdims=True) + EPS) * gdn_gn.astype(f32)
    y_gdn = (o.reshape(B, T, GDN_V).astype(h.dtype) * jax.nn.silu(gz)) @ w_br_gdn
    merged = jax.nn.sigmoid(mg_ret) * y_ret + jax.nn.sigmoid(mg_gdn) * y_gdn
    return h + merged @ w_out

def swiglu(x, wg, wu, wd):
    return (jax.nn.silu(x @ wg) * (x @ wu)) @ wd

def moe(x, router, wg, wu, wd):
    logits = (x @ router).astype(jnp.float32)
    top_logit, top_idx = lax.top_k(logits, TOP_K)
    top_w = jax.nn.softmax(top_logit, axis=-1)
    gates = jnp.sum(jax.nn.one_hot(top_idx, N_EXPERTS, dtype=jnp.float32) * top_w[..., None], axis=-2)
    y = jnp.zeros_like(x)
    for e in range(N_EXPERTS):
        y = y + gates[..., e:e + 1].astype(x.dtype) * swiglu(x, wg[e], wu[e], wd[e])
    return y

def first_inputs(seed: int = 0) -> dict:
    key = jax.random.key(seed)
    ks = jax.random.split(key, 26)
    f32 = jnp.float32

    def nrm(k, shape, fan_in):
        return jax.random.normal(k, shape, f32) * (fan_in ** -0.5)

    def gain(k, shape):
        return 1.0 + 0.02 * jax.random.normal(k, shape, f32)

    dt = jnp.exp(jax.random.uniform(ks[5], (DEPTH, GDN_HEADS), f32, np.log(1e-3), np.log(1e-1)))
    return {
        "x": jax.random.normal(ks[0], (BATCH, SEQ, D_MODEL), f32),
        "p": jax.random.normal(ks[1], (DEPTH, BATCH, SEQ, PLE_DIM), f32),
        "w_in": nrm(ks[2], (DEPTH, D_MODEL, D_IN), D_MODEL),
        "conv_w": 0.5 * jax.random.normal(ks[3], (DEPTH, CONV_WIDTH, GDN_CONV_DIM), f32),
        "a_log": jnp.log(jax.random.uniform(ks[4], (DEPTH, GDN_HEADS), f32, 1.0, 16.0)),
        "dt_bias": dt + jnp.log(-jnp.expm1(-dt)),
        "ret_gn": gain(ks[6], (DEPTH, RET_V)),
        "gdn_gn": gain(ks[7], (DEPTH, GDN_DV)),
        "w_br_ret": nrm(ks[8], (DEPTH, RET_V, D_MODEL), RET_V),
        "w_br_gdn": nrm(ks[9], (DEPTH, GDN_V, D_MODEL), GDN_V),
        "w_out": nrm(ks[10], (DEPTH, D_MODEL, D_MODEL), D_MODEL),
        "norm_mix": gain(ks[11], (DEPTH, D_MODEL)),
        "norm_ffn": gain(ks[12], (DEPTH, D_MODEL)),
        "norm_ple": gain(ks[13], (DEPTH, D_MODEL)),
        "w_ple": nrm(ks[14], (DEPTH, PLE_DIM, D_MODEL), PLE_DIM),
        "w_ple_gate": nrm(ks[15], (DEPTH, D_MODEL, D_MODEL), D_MODEL),
        "ffn_w_gate": nrm(ks[16], (N_DENSE, D_MODEL, D_FF), D_MODEL),
        "ffn_w_up": nrm(ks[17], (N_DENSE, D_MODEL, D_FF), D_MODEL),
        "ffn_w_down": nrm(ks[18], (N_DENSE, D_FF, D_MODEL), D_FF),
        "router": nrm(ks[19], (N_MOE, D_MODEL, N_EXPERTS), D_MODEL),
        "exp_w_gate": nrm(ks[20], (N_MOE, N_EXPERTS, D_MODEL, D_FF_EXPERT), D_MODEL),
        "exp_w_up": nrm(ks[21], (N_MOE, N_EXPERTS, D_MODEL, D_FF_EXPERT), D_MODEL),
        "exp_w_down": nrm(ks[22], (N_MOE, N_EXPERTS, D_FF_EXPERT, D_MODEL), D_FF_EXPERT),
        "norm_final": gain(ks[23], (D_MODEL,)),
    }

def first_block(x, p, w_in, conv_w, a_log, dt_bias, ret_gn, gdn_gn, w_br_ret, w_br_gdn, w_out,
              norm_mix, norm_ffn, norm_ple, w_ple, w_ple_gate, ffn_w_gate, ffn_w_up, ffn_w_down,
              router, exp_w_gate, exp_w_up, exp_w_down, norm_final):
    pos = jnp.arange(x.shape[1], dtype=jnp.float32)
    h = x
    for i in range(DEPTH):
        h = mixer_block(h, norm_mix[i], w_in[i], conv_w[i], a_log[i], dt_bias[i], ret_gn[i], gdn_gn[i],
                        w_br_ret[i], w_br_gdn[i], w_out[i], pos)
        u = rmsnorm(h, norm_ffn[i])
        j = i // 2
        if i % 2 == 0:
            h = h + swiglu(u, ffn_w_gate[j], ffn_w_up[j], ffn_w_down[j])
        else:
            h = h + moe(u, router[j], exp_w_gate[j], exp_w_up[j], exp_w_down[j])
        ple = p[i] @ w_ple[i]
        h = h + jax.nn.sigmoid(rmsnorm(h, norm_ple[i]) @ w_ple_gate[i]) * ple
    return rmsnorm(h, norm_final)


N_MIXERS = 2
N_A_LAYERS = (DEPTH + 1) // 2
N_B_LAYERS = DEPTH // 2

HG_EXPAND = 128
HG_HEADS = D_MODEL // HG_EXPAND
HG_KDIM = HG_EXPAND
HG_VDIM = D_MODEL // HG_HEADS
HG_CHUNK = 32

ATT_HEAD_DIM = 128
ATT_HEADS = D_MODEL // ATT_HEAD_DIM
DILATED_GROUPS = ((128, 1), (512, 4), (2048, 16))
N_GROUPS = len(DILATED_GROUPS)
ATT_QKV_COLS = N_GROUPS * 3 * ATT_HEADS * ATT_HEAD_DIM
ROPE_THETA_2 = 500000.0
ROPE_DIM = ATT_HEAD_DIM // 4

D_FF_2 = -(-(8 * D_MODEL) // (3 * 256)) * 256

NORM_EPS = 1e-6


def rms_norm(x, g):
    xf = x.astype(jnp.float32)
    y = xf * lax.rsqrt(jnp.mean(xf * xf, axis=-1, keepdims=True) + NORM_EPS)
    return (y * g.astype(jnp.float32)).astype(x.dtype)

def apply_partial_rope(t, cos, sin):
    half = ROPE_DIM // 2
    t1 = t[..., :half]
    t2 = t[..., half:ROPE_DIM]
    return jnp.concatenate([t1 * cos - t2 * sin, t2 * cos + t1 * sin, t[..., ROPE_DIM:]], axis=-1)

def hgrn2_mixer(u, w_in, lb, norm_g, w_out):
    B, S, _ = u.shape
    H, K, C = HG_HEADS, HG_KDIM, HG_CHUNK
    proj = (u @ w_in).astype(jnp.float32).reshape(B, S, 4, H, K)
    q_raw, f_raw, v, g = proj[:, :, 0], proj[:, :, 1], proj[:, :, 2], proj[:, :, 3]
    lb = lb.astype(jnp.float32).reshape(H, K)
    log_f = jnp.log(lb + (1.0 - lb) * jax.nn.sigmoid(f_raw))
    k = (1.0 - lb) * jax.nn.sigmoid(-f_raw)
    q = jax.nn.silu(q_raw)
    NC = S // C
    rs = lambda t: t.reshape(B, NC, C, H, t.shape[-1])
    q, k, v, log_f = rs(q), rs(k), rs(v), rs(log_f)
    b = jnp.cumsum(log_f, axis=2)
    q_dec = q * jnp.exp(b)
    k_inv = k * jnp.exp(-b)
    causal = jnp.tril(jnp.ones((C, C), dtype=bool))
    a = jnp.einsum('bnchk,bnshk->bnhcs', q_dec, k_inv)
    a = jnp.where(causal, a, 0.0)
    o_intra = jnp.einsum('bnhcs,bnshv->bnchv', a, v)
    b_last = b[:, :, -1:]
    k_end = k * jnp.exp(b_last - b)
    chunk_decay = jnp.exp(b_last[:, :, 0])

    def step(state, xs):
        q_c, k_c, v_c, dec = xs
        o_c = jnp.einsum('bchk,bhkv->bchv', q_c, state)
        state = dec[..., None] * state + jnp.einsum('bchk,bchv->bhkv', k_c, v_c)
        return state, o_c

    xs = (jnp.moveaxis(q_dec, 1, 0), jnp.moveaxis(k_end, 1, 0),
          jnp.moveaxis(v, 1, 0), jnp.moveaxis(chunk_decay, 1, 0))
    state0 = jnp.zeros((B, H, K, HG_VDIM), jnp.float32)
    _, o_inter = lax.scan(step, state0, xs)
    o = (o_intra + jnp.moveaxis(o_inter, 0, 1)).reshape(B, S, H, HG_VDIM)
    o = o * lax.rsqrt(jnp.mean(o * o, axis=-1, keepdims=True) + NORM_EPS)
    o = o * norm_g.astype(jnp.float32).reshape(H, HG_VDIM)
    o = o.reshape(B, S, D_MODEL) * jax.nn.silu(g.reshape(B, S, D_MODEL))
    return o.astype(u.dtype) @ w_out

def dilated_group_attention(q, k, v, window, dilation):
    B, S, H, Dh = q.shape
    L = S // dilation
    n_win = window // dilation
    blk = n_win
    nb = -(-L // blk)
    Lp = nb * blk

    def gather(t):
        t = t.reshape(B, L, dilation, H, Dh).transpose(0, 2, 1, 3, 4).reshape(B * dilation, L, H, Dh)
        t = jnp.pad(t, ((0, 0), (0, Lp - L), (0, 0), (0, 0)))
        return t.reshape(B * dilation, nb, blk, H, Dh)

    def with_prev(t):
        prev = jnp.pad(t, ((0, 0), (1, 0), (0, 0), (0, 0), (0, 0)))[:, :-1]
        return jnp.concatenate([prev, t], axis=2)

    qb = gather(q)
    kw = with_prev(gather(k))
    vw = with_prev(gather(v))
    s = jnp.einsum('bnqhd,bnkhd->bnhqk', qb, kw)
    qi = jnp.arange(blk)[:, None]
    ki = jnp.arange(2 * blk)[None, :]
    dist = blk + qi - ki
    band = (dist >= 0) & (dist <= n_win)
    has_prev = (jnp.arange(nb)[:, None, None] > 0) | (ki >= blk)[None]
    valid = band[None] & has_prev
    s = jnp.where(valid[None, :, None], s, -jnp.inf)
    m = jnp.max(s, axis=-1, keepdims=True)
    p = jnp.exp(s - m)
    z = jnp.sum(p, axis=-1, keepdims=True)
    o = jnp.einsum('bnhqk,bnkhd->bnqhd', p, vw) / jnp.swapaxes(z, 2, 3)
    lse = jnp.swapaxes((m + jnp.log(z))[..., 0], 2, 3)

    def scatter_back(t):
        rest = t.shape[3:]
        t = t.reshape(B, dilation, Lp, *rest)[:, :, :L]
        return jnp.moveaxis(t, 1, 2).reshape(B, S, *rest)

    return scatter_back(o), scatter_back(lse)

def dilated_attention_mixer(u, cos, sin, w_in, w_out):
    B, S, _ = u.shape
    proj = (u @ w_in).astype(jnp.float32).reshape(B, S, N_GROUPS, 3, ATT_HEADS, ATT_HEAD_DIM)
    scale = ATT_HEAD_DIM ** -0.5
    outs = []
    lses = []
    for gi, (window, dilation) in enumerate(DILATED_GROUPS):
        q = apply_partial_rope(proj[:, :, gi, 0], cos, sin) * scale
        k = apply_partial_rope(proj[:, :, gi, 1], cos, sin)
        v = proj[:, :, gi, 2]
        o_g, lse_g = dilated_group_attention(q, k, v, window, dilation)
        outs.append(o_g)
        lses.append(lse_g)
    wts = jax.nn.softmax(jnp.stack(lses, axis=0), axis=0)
    o = jnp.einsum('gbsh,gbshd->bshd', wts, jnp.stack(outs, axis=0))
    return o.reshape(B, S, D_MODEL).astype(u.dtype) @ w_out

def swiglu_ffn(u, w_in, w_out):
    gate, up = jnp.split(u @ w_in, 2, axis=-1)
    return (jax.nn.silu(gate) * up) @ w_out

def second_inputs(seed: int = 0) -> dict:
    key = jax.random.key(seed)
    ks = jax.random.split(key, 16)
    D = D_MODEL
    nrm = jax.random.normal
    x = nrm(ks[0], (BATCH, SEQ, D), jnp.float32)
    c = nrm(ks[1], (BATCH, D), jnp.float32)
    offset = jax.random.randint(ks[2], (BATCH, 1), 0, 1024, dtype=jnp.int32)
    positions = offset + jnp.arange(SEQ, dtype=jnp.int32)[None, :]
    ada_w = nrm(ks[3], (DEPTH, D, 6 * D), jnp.float32) * (0.5 * D ** -0.5)
    ada_b = nrm(ks[4], (DEPTH, 6 * D), jnp.float32) * 0.02
    norm_g = 1.0 + 0.05 * nrm(ks[5], (DEPTH, 4, D), jnp.float32)
    hgrn_w_in = nrm(ks[6], (N_A_LAYERS, D, 4 * D), jnp.float32) * D ** -0.5
    hgrn_lower_bounds = 1.0 + 0.5 * nrm(ks[7], (N_A_LAYERS, D), jnp.float32)
    hgrn_norm_g = 1.0 + 0.05 * nrm(ks[8], (N_A_LAYERS, D), jnp.float32)
    hgrn_w_out = nrm(ks[9], (N_A_LAYERS, D, D), jnp.float32) * D ** -0.5
    attn_w_in = nrm(ks[10], (N_B_LAYERS, D, ATT_QKV_COLS), jnp.float32) * D ** -0.5
    attn_w_out = nrm(ks[11], (N_B_LAYERS, D, D), jnp.float32) * D ** -0.5
    ffn_w_in = nrm(ks[12], (DEPTH, D, 2 * D_FF_2), jnp.float32) * D ** -0.5
    ffn_w_out = nrm(ks[13], (DEPTH, D_FF_2, D), jnp.float32) * D_FF_2 ** -0.5
    return {'x': x, 'c': c, 'positions': positions, 'ada_w': ada_w, 'ada_b': ada_b,
            'norm_g': norm_g, 'hgrn_w_in': hgrn_w_in, 'hgrn_lower_bounds': hgrn_lower_bounds,
            'hgrn_norm_g': hgrn_norm_g, 'hgrn_w_out': hgrn_w_out, 'attn_w_in': attn_w_in,
            'attn_w_out': attn_w_out, 'ffn_w_in': ffn_w_in, 'ffn_w_out': ffn_w_out}

def second_block(x, c, positions, ada_w, ada_b, norm_g, hgrn_w_in, hgrn_lower_bounds,
              hgrn_norm_g, hgrn_w_out, attn_w_in, attn_w_out, ffn_w_in, ffn_w_out):
    cond = jax.nn.silu(c)
    inv_freq = ROPE_THETA_2 ** (-jnp.arange(0, ROPE_DIM, 2, dtype=jnp.float32) / ROPE_DIM)
    ang = positions.astype(jnp.float32)[..., None] * inv_freq
    cos = jnp.cos(ang)[:, :, None, :]
    sin = jnp.sin(ang)[:, :, None, :]
    lbs = jnp.cumsum(jax.nn.softmax(hgrn_lower_bounds.astype(jnp.float32), axis=0), axis=0)
    lbs = lbs - lbs[0:1]
    h = x
    for layer in range(DEPTH):
        mod = (cond @ ada_w[layer] + ada_b[layer])[:, None, :]
        sh1, sc1, g1, sh2, sc2, g2 = jnp.split(mod, 6, axis=-1)
        u = rms_norm(h, norm_g[layer, 0]) * (1.0 + sc1) + sh1
        idx = layer // N_MIXERS
        if layer % N_MIXERS == 0:
            y = hgrn2_mixer(u, hgrn_w_in[idx], lbs[idx], hgrn_norm_g[idx], hgrn_w_out[idx])
        else:
            y = dilated_attention_mixer(u, cos, sin, attn_w_in[idx], attn_w_out[idx])
        h = h + (1.0 + g1) * rms_norm(y, norm_g[layer, 1])
        u = rms_norm(h, norm_g[layer, 2]) * (1.0 + sc2) + sh2
        y = swiglu_ffn(u, ffn_w_in[layer], ffn_w_out[layer])
        h = h + (1.0 + g2) * rms_norm(y, norm_g[layer, 3])
    return h


def setup_inputs(seed=0):
    out = dict(first_inputs(seed))
    for name, value in second_inputs(seed + 1).items():
        if name != "x":
            out[name + "_2"] = value
    return out


def reference(
    x, p, w_in, conv_w, a_log, dt_bias, ret_gn, gdn_gn, w_br_ret, w_br_gdn, w_out, norm_mix,
    norm_ffn, norm_ple, w_ple, w_ple_gate, ffn_w_gate, ffn_w_up, ffn_w_down, router, exp_w_gate,
    exp_w_up, exp_w_down, norm_final, c_2, positions_2, ada_w_2, ada_b_2, norm_g_2, hgrn_w_in_2,
    hgrn_lower_bounds_2, hgrn_norm_g_2, hgrn_w_out_2, attn_w_in_2, attn_w_out_2, ffn_w_in_2,
    ffn_w_out_2,
):
    x = first_block(
        x, p, w_in, conv_w, a_log, dt_bias, ret_gn, gdn_gn, w_br_ret, w_br_gdn, w_out, norm_mix,
        norm_ffn, norm_ple, w_ple, w_ple_gate, ffn_w_gate, ffn_w_up, ffn_w_down, router,
        exp_w_gate, exp_w_up, exp_w_down, norm_final,
    )
    return second_block(
        x, c_2, positions_2, ada_w_2, ada_b_2, norm_g_2, hgrn_w_in_2, hgrn_lower_bounds_2,
        hgrn_norm_g_2, hgrn_w_out_2, attn_w_in_2, attn_w_out_2, ffn_w_in_2, ffn_w_out_2,
    )


_drawn_inputs = setup_inputs


def setup_inputs(seed=0):
    import zlib

    import numpy as np

    out = dict(_drawn_inputs(seed))
    spreads = {}
    factors = {'norm_ple': 8.0}
    for name, (base, spread) in spreads.items():
        noise = np.random.default_rng([zlib.crc32(name.encode()), seed]).standard_normal(out[name].shape)
        drawn = base * np.exp(spread * noise) if base else spread * noise
        out[name] = jnp.asarray(drawn.astype(out[name].dtype))
    for name, factor in factors.items():
        out[name] = (out[name] * factor).astype(out[name].dtype)
    return out
```

```python
from contextlib import ExitStack

import numpy as np

import concourse.bass as bass
from concourse import mybir

F32 = mybir.dt.float32
U32 = mybir.dt.uint32
I32 = mybir.dt.int32
ALU = mybir.AluOpType
ACT = mybir.ActivationFunctionType
AX = mybir.AxisListType.X

P = 128
T = 256
TT = T // P
D = 1024
KT = D // P
DEPTH = 2
EPS = 1e-6
RET_H = 4
GH = 8
HALF = 4
EXPERTS = 8
FE = 1408 // P
DENSE_E = 2816 // 1408
GROUPS = (4, 4, 3)
OFF_RQ, OFF_RK, OFF_RV, OFF_RG = 0, 512, 1024, 2048
OFF_GQKV, OFF_GZ, OFF_GA, OFF_MR, OFF_MG = 3072, 6144, 7168, 7184, 8208
HG_C = 32
DIL = (1, 4, 16)
R = 6
SLOT = 2048
NEG = -1.0e30


def shape_constants():
    i = np.arange(P)
    f = np.float32
    up = (i[:, None] <= i[None, :]).astype(f)
    sup = (i[:, None] < i[None, :]).astype(f)
    one = np.ones((P, P), f)
    c = {"ident": np.eye(P, dtype=f),
         "mI": np.concatenate([up, one, up], 1), "mS": np.concatenate([sup, one, sup], 1)}
    lg = np.log1p(-np.exp2(-5.0 - np.arange(RET_H)))
    for h in range(RET_H):
        rel = i[None, :] - i[:, None]
        dg = np.where(rel >= 0, np.exp(np.maximum(rel, 0) * lg[h]), 0.0)
        off = np.exp((rel + P) * lg[h])
        c[f"ret{h}"] = (np.concatenate([dg, off, dg], 1) * P ** -0.5).astype(f)
    for n in range(7):
        b = 1 << n
        same = (i[:, None] // (2 * b)) == (i[None, :] // (2 * b))
        c[f"mg{n}"] = (same & ((i[:, None] // b) % 2 == 0) & ((i[None, :] // b) % 2 == 1)).astype(f)
    for n, d in enumerate(DIL):
        diff = i[:, None] - i[None, :]
        dg = (diff >= 0) & (diff % d == 0)
        off = (diff % d == 0) & (((diff + P) // d <= P))
        c[f"at{n}"] = np.where(np.concatenate([dg, off, dg], 1), 0.0, NEG).astype(f)
    c["hg"] = ((i[:, None] <= i[None, :]) & (i[:, None] // HG_C == i[None, :] // HG_C)).astype(f)
    c["reset"] = np.tile((np.arange(T) % HG_C != 0).astype(f), (P, 1))
    for name, half in (("rot1", 64), ("rot2", 16)):
        m = np.zeros((P, P), f)
        for k in range(half):
            m[k + half, k] = -1.0
            m[k, k + half] = 1.0
        c[name] = m
    half = 64
    fr = (np.float32(10000.0) ** (-np.arange(half, dtype=f) / np.float32(half))).astype(f)
    ang = (np.arange(T, dtype=f)[None, :] * fr[:, None]).astype(f).astype(np.float64)
    ang = np.concatenate([ang, ang], 0)
    c["cos1"], c["sin1"] = np.cos(ang).astype(f), np.sin(ang).astype(f)
    fr = (np.float32(500000.0) ** (-np.arange(0, 32, 2, dtype=f) / np.float32(32))).astype(f)
    c["freq2"] = np.concatenate([fr, fr, np.zeros(96, f)])[:, None]
    c["eps"] = np.full((P, 1), EPS, f)
    c["mhalf"] = np.full((P, 16), -0.5, f)
    c["halfpi"] = np.full((P, 1), np.pi / 2, f)
    return c


def cols(v):
    return v.reshape(-1, P).T


def host_layout(x):
    b = shape_constants()
    for l in range(DEPTH):
        for n in ("norm_mix", "norm_ffn", "norm_ple"):
            b[f"{n}{l}"] = cols(x[n][l])
        b[f"ret_gn{l}"] = cols(x["ret_gn"][l])
        b[f"gdn_gn{l}"] = cols(x["gdn_gn"][l])
        b[f"conv{l}"] = x["conv_w"][l].reshape(4, 24, P).transpose(2, 1, 0).reshape(P, 96)
        b[f"alog{l}"] = np.broadcast_to(x["a_log"][l][None, :], (P, GH))
        b[f"dtb{l}"] = np.broadcast_to(x["dt_bias"][l][None, :], (P, GH))
        b[f"wab{l}"] = x["w_in"][l][:, OFF_GA:OFF_MR].reshape(KT, P, 16).transpose(1, 0, 2).reshape(P, P)
        b[f"pT{l}"] = x["p"][l, 0].T.reshape(2, P, T).transpose(1, 0, 2).reshape(P, 2 * T)
        b[f"adab{l}"] = cols(x["ada_b_2"][l])
        for j in range(4):
            b[f"ng{l}{j}"] = cols(x["norm_g_2"][l, j])
    b["router"] = x["router"][0].reshape(KT, P, EXPERTS).transpose(1, 0, 2).reshape(P, KT * EXPERTS)
    b["norm_final"] = cols(x["norm_final"])
    b["cond"] = cols(x["c_2"][0])
    b["hglb"] = cols(x["hgrn_lower_bounds_2"][0])
    b["hgng"] = cols(x["hgrn_norm_g_2"][0])
    return b


def build(nc, columns, ins, out, unit_freed):
    ctx = ExitStack()
    with ctx:
        def sb(name, shape, dt=F32):
            return ctx.enter_context(nc.sbuf_tensor(name, shape, dt))

        sems = []

        def sem(name):
            sems.append(ctx.enter_context(nc.semaphore(name)))
            return sems[-1]

        NCOL = ins["small"].shape[1]
        small = sb("small", [P, NCOL])
        ring = sb("ring", [P, R, SLOT])
        h = sb("h", [P, TT, D])
        xn = sb("xn", [P, TT, D])
        uT = sb("uT", [P, KT, T])
        work = sb("work", [P, 26 * 1024])
        tiny = sb("tiny", [P, 660])
        ps = [ctx.enter_context(nc.psum_tensor(f"ps{i}", [P, 1024], F32)) for i in range(4)]

        def col(name, a=0, b=None):
            o, w = columns[name]
            return small[:, o + a:o + (w if b is None else b)]

        def area(k0, n, **shape):
            v = work[:, int(k0 * 1024):int(k0 * 1024) + n]
            return v

        ident, ones = col("ident"), col("mI", P, T)
        triu = col("mI", 0, P)
        triu_ones = col("mI", 0, T)
        eps, mhalf = col("eps"), col("mhalf")

        used = [0]

        def small_tile(n):
            used[0] += n
            assert used[0] <= 660
            return tiny[:, used[0] - n:used[0]]

        ssum, msq, rstd = small_tile(2), small_tile(2), small_tile(2)
        hsum, hms, hrs = small_tile(16), small_tile(16), small_tile(16)
        bst, bag, brs = small_tile(12), small_tile(4), small_tile(2)
        gcol, beta = small_tile(16), small_tile(16)
        gx, gab, gab2 = small_tile(16), small_tile(16), small_tile(16)
        gcn, nea = small_tile(16), small_tile(8)
        gates, lg8, sel8 = (small_tile(16) for _ in range(3))
        nm1, e8, es = small_tile(2), small_tile(16), small_tile(2)
        cond, mod = small_tile(8), small_tile(48)
        gmix, gmix2, grow, grow2 = small_tile(8), small_tile(8), small_tile(8), small_tile(8)
        lbe, lbr, lbs, oml = small_tile(8), small_tile(8), small_tile(8), small_tile(8)

        small_in, x_in, pos_in = sem("small_in"), sem("x_in"), sem("pos_in")
        slab_in = [sem(f"slab_in{i}") for i in range(R)]
        slab_used = sem("slab_used")
        psum_full = sem("psum_full")
        psum_read = sem("psum_read")
        act_step, dve_step, pool_step = sem("act_step"), sem("dve_step"), sem("pool_step")
        h_new = sem("h_new")
        ss_done, ms_done, rstd_done = sem("ss_done"), sem("ms_done"), sem("rstd_done")
        nat_ready, t_ready_lo, t_ready_hi = sem("nat_ready"), sem("t_ready_lo"), sem("t_ready_hi")
        rope_in, rope_cos, rope_out = sem("rope_in"), sem("rope_cos"), sem("rope_out")
        rope_tab = sem("rope_tab")
        ret_v, ret_g, ret_s, ret_var, ret_rs = (sem(n) for n in ("ret_v", "ret_g", "ret_s", "ret_var", "ret_rs"))
        conv_in, conv_acc, conv_out, gz_out = sem("conv_in"), sem("conv_acc"), sem("conv_out"), sem("gz_out")
        ab_x, ab_abs, ab_soft, ab_bc, g_ready = sem("ab_x"), sem("ab_abs"), sem("ab_soft"), sem("ab_bc"), sem("g_ready")
        sq_out, nrm_root, qk_norm = sem("sq_out"), sem("nrm_root"), sem("qk_norm")
        v_beta, dec_arg, dec_exp, dec_mask, kb_out, a_out = (
            sem(n) for n in ("v_beta", "dec_arg", "dec_exp", "dec_mask", "kb_out", "a_out"))
        c_out, x_out, m_out, u_out, r_out = (sem(n) for n in ("c_out", "x_out", "m_out", "u_out", "r_out"))
        hn_sq, hn_ms, hn_rs = sem("hn_sq"), sem("hn_ms"), sem("hn_rs")
        sig_out, merged_out = sem("sig_out"), sem("merged_out")
        row_rhs, row_out = sem("row_rhs"), sem("row_out")
        silu_out, hid_out, gate_b = sem("silu_out"), sem("hid_out"), sem("gate_b")
        rt_l, rt_nm, rt_e = sem("rt_l"), sem("rt_nm"), sem("rt_e")
        cond_out, mod_out, y_out = sem("cond_out"), sem("mod_out"), sem("y_out")
        ada_in, ada_sum = [sem(f"ada_in{i}") for i in range(2)], sem("ada_sum")
        hg_q, hg_f, hg_lb, hg_ff, hg_ln, hg_b, hg_exp, hg_mul, hg_nat, hg_a, hg_s = (
            sem(n) for n in ("hg_q", "hg_f", "hg_lb", "hg_ff", "hg_ln", "hg_b", "hg_exp", "hg_mul", "hg_nat", "hg_a", "hg_s"))
        at_v, at_s, at_p, at_t, at_o, at_lse, at_w, at_part = (
            sem(n) for n in ("at_v", "at_s", "at_p", "at_t", "at_o", "at_lse", "at_w", "at_part"))
        y_zero, hid_raw, gate_row, ple_out, plg_out, hg_v, hg_gt, hn_gated, tab_sin = (
            sem(n) for n in ("y_zero", "hid_raw", "gate_row", "ple_out", "plg_out", "hg_v", "hg_gt", "hn_gated", "tab_sin"))
        out_done = sem("out_done")

        block = ctx.enter_context(nc.Block())

        T_ORDER = []
        S_ORDER = []
        for l in range(DEPTH):
            T_ORDER += [f"mix{l}", f"oret{l}", f"ogdn{l}", f"ffn{l}", f"ple{l}"]
            S_ORDER += [f"mix{l}", f"ffn{l}", f"ple{l}"]
        S_ORDER += ["final"]
        for l in range(DEPTH):
            T_ORDER += [f"smix{l}", f"so{l}", f"sffn{l}"]
            S_ORDER += [f"smix{l}", f"spost{l}", f"sffn{l}", f"spostf{l}"]
        ROWS = ["final", "post0", "postf0", "post1", "postf1"]
        H_ORDER = ["mix0", "ffn0", "ple0", "mix1", "ffn1", "ple1", "final", "smix0", "sffn0", "smix1", "sffn1"]

        def turned(name):
            return T_ORDER.index(name) + 1

        slabs = []

        def slab_list():
            def wide(name, w, k0, n, c0, c):
                slabs.append((name, w[k0:k0 + n * P, c0:c0 + c].rearrange("(k p) c -> p k c", p=P), n, c))

            def linear(name, w, c0, width, kt=KT):
                for j in range(width // 512):
                    for half in range(kt // 4):
                        wide(name, w, half * 512, 4, c0 + j * 512, 512)

            def ffn(name, e_count):
                slabs.append((name, None, e_count, 0))

            for l in range(DEPTH):
                w = ins["w_in"][l]
                linear(f"rqk{l}", w, OFF_RQ, 1024)
                linear(f"rv{l}", w, OFF_RV, 1024)
                linear(f"rg{l}", w, OFF_RG, 1024)
                linear(f"gqkv{l}", w, OFF_GQKV, 3072)
                linear(f"gz{l}", w, OFF_GZ, 1024)
                for j in range(2):
                    linear(f"mgret{l}", w, OFF_MR + j * 512, 512)
                    linear(f"brret{l}", ins["w_br_ret"][l], j * 512, 512)
                linear(f"mggdn{l}", w, OFF_MG, D)
                linear(f"brgdn{l}", ins["w_br_gdn"][l], 0, D)
                linear(f"wo{l}", ins["w_out"][l], 0, D)
                ffn(f"ffn{l}", DENSE_E if l % 2 == 0 else EXPERTS)
                wide(f"ple{l}", ins["w_ple"][l], 0, 2, 0, D)
                linear(f"plg{l}", ins["w_ple_gate"][l], 0, D)
            for l in range(DEPTH):
                if l % 2 == 0:
                    w = ins["hgrn_w_in_2"][0]
                    linear("hq", w, 0, D)
                    linear("hf", w, D, D)
                    linear("hv", w, 2 * D, D)
                    linear("hgt", w, 3 * D, D)
                    linear("ho", ins["hgrn_w_out_2"][0], 0, D)
                else:
                    w = ins["attn_w_in_2"][0]
                    for g in range(3):
                        for j in range(3):
                            linear(f"at{g}{j}", w, (3 * g + j) * D, D)
                    linear("ao", ins["attn_w_out_2"][0], 0, D)
                ffn(f"sffn{l}", DENSE_E)

        slab_list()

        def ffn_weights(name):
            F = FE * P
            if name == "ffn0":
                g, u, d = ins["ffn_w_gate"][0], ins["ffn_w_up"][0], ins["ffn_w_down"][0]
            elif name == "ffn1":
                g, u, d = ins["exp_w_gate"][0], ins["exp_w_up"][0], ins["exp_w_down"][0]
                return (lambda e, r, c, n: g[bass.ds(e, 1), r:r + 512, c:c + n],
                        lambda e, r, c, n: u[bass.ds(e, 1), r:r + 512, c:c + n],
                        lambda e, r, n: d[bass.ds(e, 1), r:r + n, :])
            else:
                l = int(name[-1])
                w = ins["ffn_w_in_2"][l]
                g, u, d = w[:, 0:2 * F], w[:, 2 * F:4 * F], ins["ffn_w_out_2"][l]
            g, u = (w.rearrange("k (e c) -> e k c", e=DENSE_E) for w in (g, u))
            d = d.rearrange("(e k) c -> e k c", e=DENSE_E)
            return (lambda e, r, c, n: g[bass.ds(e, 1), r:r + 512, c:c + n],
                    lambda e, r, c, n: u[bass.ds(e, 1), r:r + 512, c:c + n],
                    lambda e, r, n: d[bass.ds(e, 1), r:r + n, :])

        def ffn_slabs():
            first = [sum(GROUPS[:g]) for g in range(3)]
            up = lambda g: [("g", g, 0), ("g", g, 1), ("u", g, 0), ("u", g, 1)]
            down = lambda g: [("d", first[g] + t, min(2, GROUPS[g] - t)) for t in range(0, GROUPS[g], 2)]
            return up(0) + up(1) + down(0) + up(2) + down(1) + down(2)

        PER_E = len(ffn_slabs())
        assert PER_E % R == 0


        slot_of, pair_before, holds = {}, {}, {}
        next_slot, ring_pairs = [0], [4]
        freed = dict(unit_freed)
        freed_now = {}
        by_name = {s_.name: s_ for s_ in sems}
        name_of = {id(s_): s_.name for s_ in sems}
        slab_n = [0]
        steps = {"act": 0, "dve": 0, "pool": 0}

        ticks = {}
        last = [None]
        full_at = {}
        current = [None]

        def tick(s_, by=1):
            ticks[id(s_)] = ticks.get(id(s_), 0) + by
            last[0] = (s_, ticks[id(s_)])
            if s_ is psum_full:
                full_at[current[0]] = last[0]
            return s_

        def take_unit(pe, name, slot=None):
            if slot is None:
                slot = next_slot[0] % ring_pairs[0]
                next_slot[0] = slot + 1
            slot_of[name], pair_before[name] = slot, holds.get(slot)
            holds[slot] = current[0] = name
            if pair_before[name] in freed:
                k_, v_ = freed[pair_before[name]]
                pe.wait_ge(by_name[k_], v_)
            return ps[slot]

        def filled(name):
            full_at[name] = last[0]

        def full(eng, name):
            eng.wait_ge(*full_at[name])
            return ps[slot_of[name]]

        def free(name):
            freed_now[name] = (name_of[id(last[0][0])], last[0][1])

        def astep(act, i_):
            steps["act"] += 1
            i_.then_inc(tick(act_step), 1)
            act.wait_ge(act_step, steps["act"])

        def dstep(dve, i_):
            steps["dve"] += 1
            i_.then_inc(tick(dve_step), 1)
            dve.wait_ge(dve_step, steps["dve"])

        def pstep(pool, i_):
            steps["pool"] += 1
            i_.then_inc(tick(pool_step), 1)
            pool.wait_ge(pool_step, steps["pool"])

        def take_slab(pe, name):
            n = slab_n[0]
            assert slabs[n][0] == name, (slabs[n][0], name)
            slab_n[0] += 1
            m = n + extra[0]
            _, _, kt, c = slabs[n]
            pe.wait_ge(slab_in[m % R], 16 * (m // R + 1))
            return ring[:, m % R, 0:kt * c].rearrange("p (k c) -> p k c", c=c)

        extra = [0]

        def linear_t(pe, slab, unit, src=uT):
            acc = take_unit(pe, unit)
            for half in range(2):
                w = take_slab(pe, slab)
                for m in range(4):
                    mm = linear_t_tile(pe, acc, w, half, m, src)
                mm.then_inc(tick(slab_used), 1)
            filled(unit)

        def linear_t_tile(pe, acc, w, half, m, src):
            for k in range(4):
                mm = pe.matmul(acc[:, m * T:(m + 1) * T], w[:, k, m * P:(m + 1) * P],
                               src[:, half * 4 + k, :], start=(half == 0 and k == 0 and m % 2 == 0),
                               stop=(half == 1 and k == 3), skip_group_check=True)
            return mm

        def linear_n(pe, slab, unit, src=uT, halves=2):
            acc = take_unit(pe, unit)
            for half in range(halves):
                w = take_slab(pe, slab)
                for t in range(TT):
                    for k in range(4):
                        mm = pe.matmul(acc[:, t * 512:(t + 1) * 512], src[:, half * 4 + k, t * P:(t + 1) * P],
                                       w[:, k, :], start=(half == 0 and k == 0), stop=(half == halves - 1 and k == 3))
                mm.then_inc(tick(slab_used), 1)
            filled(unit)

        def stat_act(act, name, src):
            for t in range(TT):
                act.activation(junk[:, 0:D], src[:, t, :], ACT.Square, accum_out=ssum[:, t:t + 1]).then_inc(tick(ss_done), 1)
                act.wait_ge(ss_done, 2 * S_ORDER.index(name) + t + 1)

        def stat_dve(dve, name):
            n = S_ORDER.index(name)
            dve.wait_ge(ss_done, 2 * n + 2)
            dve.tensor_scalar(msq, ssum, 1.0 / D, EPS, ALU.mult, ALU.add).then_inc(tick(ms_done), 1)
            dve.wait_ge(rstd_done, n + 1)

        def stat_pool(pool, name):
            n = S_ORDER.index(name)
            pool.wait_ge(ms_done, n + 1)
            pool.tensor_tensor(rstd, msq, mhalf[:, 0:2], ALU.pow).then_inc(tick(rstd_done), 1)

        def turn_pe(pe, name, src):
            pe.wait_ge(nat_ready, T_ORDER.index(name) + 1)
            for half in range(2):
                acc = take_unit(pe, f"t{half}{name}")
                for k in range(4):
                    for t in range(TT):
                        a = (half * 4 + k) * P
                        mm = pe.transpose(acc[:, k * T + t * P:k * T + (t + 1) * P], src[:, t, a:a + P], ident)
                mm.then_inc(tick(psum_full), 1)

        def turn_dve(dve, name, dst, gain, shift=None, same=False):
            unit = f"t0{name}"
            acc = full(dve, unit)
            for k in range(4):
                g = gain[:, 0:1] if same else gain[:, k:k + 1]
                if shift is None:
                    i_ = dve.tensor_scalar(dst[:, k, :], acc[:, k * T:(k + 1) * T], g, None, ALU.mult)
                else:
                    i_ = dve.tensor_scalar(dst[:, k, :], acc[:, k * T:(k + 1) * T], g, shift[:, k:k + 1], ALU.mult, ALU.add)
            i_.then_inc(tick(t_ready_lo), 1)
            free(unit)

        def turn_act(act, name, dst, gain, shift=None, same=False):
            unit = f"t1{name}"
            acc = full(act, unit)
            for k in range(4):
                g = gain[:, 0:1] if same else gain[:, 4 + k:5 + k]
                b = 0.0 if shift is None else shift[:, 4 + k:5 + k]
                i_ = act.activation(dst[:, 4 + k, :], acc[:, k * T:(k + 1) * T], ACT.Identity, bias=b, scale=g)
            i_.then_inc(tick(t_ready_hi), 1)
            free(unit)

        def norm_pe(pe, name):
            turn_pe(pe, name, xn)
            pe.wait_ge(t_ready_lo, turned(name))
            pe.wait_ge(t_ready_hi, turned(name))

        def norm_act(act, name, gain, shift=None):
            if name == "mix0":
                act.wait_ge(x_in, 16)
            else:
                act.wait_ge(h_new, H_BEFORE[name])
            stat_act(act, name, h)
            if shift is not None:
                act.wait_ge(mod_out, MOD_BEFORE[name])
            turn_act(act, name, uT, gain, shift)

        def norm_dve(dve, name, gain, shift=None):
            stat_dve(dve, name)
            for t in range(TT):
                i_ = dve.tensor_scalar(xn[:, t, :], h[:, t, :], rstd[:, t:t + 1], None, ALU.mult)
            i_.then_inc(tick(nat_ready), 1)
            turn_dve(dve, name, uT, gain, shift)

        H_BEFORE = {"ffn0": 1, "ple0": 2, "mix1": 3, "ffn1": 4, "ple1": 5, "final": 6,
                    "smix0": 7, "sffn0": 8, "smix1": 9, "sffn1": 10}
        MOD_BEFORE = {"smix0": 1, "sffn0": 1, "smix1": 2, "sffn1": 2}
        junk = area(25, 1024)

        rope_x = [area(24 - 4 - k, 1024) for k in range(2)]
        rope_tmp = area(22, 1024)

        def rope_pe(pe, n, unit, rot):
            pe.wait_ge(rope_in, n + 1)
            acc = take_unit(pe, unit)
            for j in range(2):
                mm = pe.matmul(acc[:, j * 512:(j + 1) * 512], rot, rope_x[n % 2][:, j * 512:(j + 1) * 512],
                               start=True, stop=True)
            mm.then_inc(tick(psum_full), 1)

        def rope_act(act, n, unit):
            acc = full(act, unit)
            if n >= 2:
                act.wait_ge(rope_out, n - 1)
            i_ = act.activation(rope_x[n % 2], acc[:, :], ACT.Copy)
            i_.then_inc(tick(rope_in), 1)
            free(unit)

        def rope_pool(pool, n, dst, cos):
            pool.wait_ge(rope_in, n + 1)
            pool.tensor_tensor(dst.rearrange("p (a t) -> p a t", a=4), rope_x[n % 2].rearrange("p (a t) -> p a t", a=4),
                               cos.unsqueeze(1).broadcast_to([P, 4, T]), ALU.mult).then_inc(tick(rope_cos), 1)

        def rope_dve(dve, n, unit, dst, sin):
            acc = full(dve, unit)
            if n:
                dve.wait_ge(rope_out, n)
            i_ = dve.tensor_tensor(rope_tmp.rearrange("p (a t) -> p a t", a=4), acc[:, :].rearrange("p (a t) -> p a t", a=4),
                                   sin.unsqueeze(1).broadcast_to([P, 4, T]), ALU.mult)
            dstep(dve, i_)
            free(unit)
            dve.wait_ge(rope_cos, n + 1)
            dve.tensor_tensor(dst, dst, rope_tmp, ALU.add).then_inc(tick(rope_out), 1)

        qk_ret = area(0, 2048)
        v_ret = area(2, 2048).rearrange("p (t d) -> p t d", t=TT)
        merged = area(2, 2048).rearrange("p (k t) -> p k t", t=T)
        o_ret = area(4, 2048).rearrange("p (t d) -> p t d", t=TT)
        o_gdn = area(6, 2048).rearrange("p (t d) -> p t d", t=TT)
        cv = area(8, 6144).rearrange("p (k t) -> p k t", t=T)
        vb = area(14, 2048).rearrange("p (t d) -> p t d", t=TT)
        oT = xn.rearrange("p t d -> p (t d)").rearrange("p (k t) -> p k t", t=T)
        s_ret = [area(16 + k * 0.375, 384) for k in range(2)]
        o_tmp = area(17, 512)
        cin = [area(18 + 1.25 * k, 4 * 259).rearrange("p (a t) -> p a t", a=4) for k in range(2)]
        cacc = [area(20.5 + k, 1024).rearrange("p (a t) -> p a t", a=4) for k in range(2)]
        sq = [area(16 + k, 1024) for k in range(2)]
        root = area(24, 1024)
        X = area(0, 1024).rearrange("p (n c) -> p n c", c=P)
        XT = area(1, 1024).rearrange("p (n c) -> p n c", c=P)
        AT = area(12, 1536).rearrange("p (n c) -> p n c", c=384)
        QK = area(16, 1536).rearrange("p (n c) -> p n c", c=384)
        CT = area(18, 1024).rearrange("p (n c) -> p n c", c=P)
        MS = area(19, 1024).rearrange("p (n c) -> p n c", c=P)
        dec = [area(20 + 0.375 * k, 384) for k in range(2)]
        decI = [area(20.75 + 0.375 * k, 384) for k in range(2)]
        decS = [area(21.5 + 0.375 * k, 384) for k in range(2)]
        kb = [area(22.25 + 0.25 * k, 256) for k in range(2)]
        bc = [area(22.75 + 0.5 * k, 512).rearrange("p (n c) -> p n c", c=P) for k in range(2)]
        U1, U2 = area(23.75, 512), area(24.25, 512)
        hsqr = area(19, 1024)
        sg = [area(k, 1024) for k in (25, 25, 8, 10)]
        btmp = area(18, 1024)
        gbeta = small_tile(32).rearrange("p (n c) -> p n c", c=4)

        RET_ORDER = ["s0", "s1", "o0", "s2", "o1", "s3", "o2", "o3"]

        def mixer_pe(pe, l):
            norm_pe(pe, f"mix{l}")
            for j in range(2):
                linear_t(pe, f"rqk{l}", f"rqk{l}{j}")
            for j in range(2):
                linear_n(pe, f"rv{l}", f"rv{l}{j}")
                rope_pe(pe, 2 * l + j, f"rope{l}{j}", col("rot1"))
            for j in range(2):
                linear_n(pe, f"rg{l}", f"rg{l}{j}")
            pe.wait_ge(rope_out, 2 * l + 2)
            pe.wait_ge(ret_v, 2 * l + 2)
            for what in RET_ORDER:
                n = int(what[1])
                acc = take_unit(pe, f"ret{what}{l}")
                if what[0] == "s":
                    q, k = (qk_ret[:, (4 * a + n) * T:(4 * a + n + 1) * T] for a in range(2))
                    pe.matmul(acc[:, 0:T], k[:, 0:P], q, start=True, stop=True)
                    mm = pe.matmul(acc[:, T:384], k[:, P:T], q[:, P:T], start=True, stop=True)
                else:
                    pe.wait_ge(ret_s, 4 * l + n + 1)
                    s = s_ret[n % 2]
                    v = v_ret[:, :, n * 256:(n + 1) * 256]
                    pe.matmul(acc[:, 0:256], s[:, 0:P], v[:, 0, :], start=True, stop=True)
                    pe.matmul(acc[:, 256:512], s[:, P:T], v[:, 0, :], start=True, stop=False)
                    mm = pe.matmul(acc[:, 256:512], s[:, T:384], v[:, 1, :], start=False, stop=True)
                mm.then_inc(tick(psum_full), 1)
                if what == "o1":
                    linear_t(pe, f"gqkv{l}", f"gqkv{l}0")
            for j in range(6):
                if j:
                    linear_t(pe, f"gqkv{l}", f"gqkv{l}{j}")
                if j < 2:
                    continue
                pe.wait_ge(sq_out, 4 * l + j - 1)
                acc = take_unit(pe, f"nrm{l}{j - 2}")
                for i in range(2):
                    mm = pe.matmul(acc[:, i * 512:(i + 1) * 512], ones, sq[j % 2][:, i * 512:(i + 1) * 512],
                                   start=True, stop=True)
                mm.then_inc(tick(psum_full), 1)
            acc = take_unit(pe, f"ab{l}")
            wab = col(f"wab{l}").rearrange("p (k c) -> p k c", c=16)
            for t in range(TT):
                for k in range(KT):
                    mm = pe.matmul(acc[:, t * 16:(t + 1) * 16], uT[:, k, t * P:(t + 1) * P], wab[:, k, :],
                                   start=(k == 0), stop=(k == KT - 1))
            mm.then_inc(tick(psum_full), 1)
            for j in range(2):
                linear_n(pe, f"gz{l}", f"gz{l}{j}")
            pe.wait_ge(conv_out, 6 * l + 6)
            for t in range(TT):
                acc = take_unit(pe, f"v{l}{t}")
                for n in range(GH):
                    mm = pe.transpose(acc[:, n * P:(n + 1) * P], cv[:, 16 + n, t * P:(t + 1) * P], ident)
                mm.then_inc(tick(psum_full), 1)
            pe.wait_ge(g_ready, l + 1)
            acc = take_unit(pe, f"gc{l}")
            g0, g1 = gbeta[:, :, 0], gbeta[:, :, 1]
            pe.matmul(acc[:, 0:GH], triu, g0, start=True, stop=True)
            pe.matmul(acc[:, GH:2 * GH], ones, g0, start=True, stop=False)
            mm = pe.matmul(acc[:, GH:2 * GH], triu, g1, start=False, stop=True)
            mm.then_inc(tick(psum_full), 1)
            turn_pe(pe, f"oret{l}", o_ret)
            next_slot[0], ring_pairs[0] = 0, 3
            for half in range(2):
                solve_pe(pe, l, half)
            next_slot[0], ring_pairs[0] = 0, 4
            turn_pe(pe, f"ogdn{l}", o_gdn)
            pe.wait_ge(t_ready_lo, turned(f"ogdn{l}"))
            pe.wait_ge(t_ready_hi, turned(f"ogdn{l}"))
            for j in range(2):
                linear_t(pe, f"brgdn{l}", f"brgdn{l}{j}", oT)
            pe.wait_ge(merged_out, 4 * l + 4)
            for j in range(2):
                linear_n(pe, f"wo{l}", f"wo{l}{j}", merged)

        BESIDE = (("mgret", 0), ("brret", 0), ("mgret", 1), ("brret", 1), ("mggdn", 0), ("mggdn", 1))
        beside_slab = [None]

        def beside_pe(pe, l, i):
            name, j = BESIDE[i // 8]
            part, m = i // 4 % 2, i % 4
            unit = f"{name}{l}{j}"
            src = oT if name == "brret" else uT
            if name == "brret" and i % 16 == 8 and j == 0:
                pe.wait_ge(t_ready_lo, turned(f"oret{l}"))
                pe.wait_ge(t_ready_hi, turned(f"oret{l}"))
            if i % 8 == 0:
                take_unit(pe, unit, 3)
            if m == 0:
                beside_slab[0] = take_slab(pe, f"{name}{l}")
            mm = linear_t_tile(pe, ps[slot_of[unit]], beside_slab[0], part, m, src)
            if m == 3:
                mm.then_inc(tick(slab_used), 1)
                filled(unit)

        def solve_pe(pe, l, half):
            def spread(n):
                i = l * GH + n
                pe.wait_ge(ab_bc, i + 1)
                acc = take_unit(pe, f"sp{l}{n}")
                b = bc[n % 2]
                pe.matmul(acc[:, 0:T], b[:, 0, :], triu_ones, start=True, stop=False)
                pe.matmul(acc[:, P:T], b[:, 1, :], triu, start=False, stop=True)
                pe.matmul(acc[:, 512:640], b[:, 2, :], ident, start=True, stop=True)
                pe.matmul(acc[:, 640:768], b[:, 3, :], ident, start=True, stop=True).then_inc(tick(psum_full), 1)

            def gram(n):
                i = l * GH + n
                pe.wait_ge(kb_out, i + 1)
                acc = take_unit(pe, f"gr{l}{n}")
                k, q = cv[:, 8 + n, :], cv[:, n, :]
                pe.matmul(acc[:, 0:T], k[:, 0:P], kb[n % 2], start=True, stop=True)
                pe.matmul(acc[:, T:384], k[:, P:T], kb[n % 2][:, P:T], start=True, stop=True)
                pe.matmul(acc[:, 512:768], k[:, 0:P], q, start=True, stop=True)
                pe.matmul(acc[:, 768:896], k[:, P:T], q[:, P:T], start=True, stop=True).then_inc(tick(psum_full), 1)

            if half == 0:
                pe.wait_ge(qk_norm, 4 * l + 4)
            h0 = half * HALF
            spread(h0)
            for n in range(h0, h0 + HALF):
                if n + 1 < h0 + HALF:
                    spread(n + 1)
                gram(n)
                for i in range(2):
                    beside_pe(pe, l, 24 * half + 2 * (n - h0) + i)
            for i in range(8, 12):
                beside_pe(pe, l, 24 * half + i)
            s = 2 * l + half
            pe.wait_ge(x_out, 13 * s + 1)
            acc = take_unit(pe, f"x0{l}{half}")
            for i in range(8):
                mm = pe.transpose(acc[:, i * P:(i + 1) * P], XT[:, i, :], ident)
            mm.then_inc(tick(psum_full), 1)
            for lev in range(1, 7):
                pe.wait_ge(c_out, 7 * s + lev + 1)
                pe.wait_ge(x_out, 13 * s + 2 * lev)
                acc = take_unit(pe, f"m{lev}{l}{half}")
                for i in range(8):
                    mm = pe.matmul(acc[:, i * P:(i + 1) * P], CT[:, i, :], X[:, i, :], start=True, stop=True)
                mm.then_inc(tick(psum_full), 1)
                beside_pe(pe, l, 24 * half + 10 + 2 * lev)
                pe.wait_ge(m_out, 6 * s + lev)
                if lev < 6:
                    acc = take_unit(pe, f"p{lev}{l}{half}")
                    for i in range(8):
                        mm = pe.matmul(acc[:, i * P:(i + 1) * P], XT[:, i, :], MS[:, i, :], start=True, stop=True)
                    mm.then_inc(tick(psum_full), 1)
                acc = take_unit(pe, f"q{lev}{l}{half}")
                for i in range(8):
                    mm = pe.matmul(acc[:, i * P:(i + 1) * P], MS[:, i, :], XT[:, i, :], start=True, stop=True)
                mm.then_inc(tick(psum_full), 1)
                beside_pe(pe, l, 24 * half + 11 + 2 * lev)
            pe.wait_ge(x_out, 13 * s + 13)
            acc = take_unit(pe, f"u1{l}{half}")
            for i in range(HALF):
                mm = pe.matmul(acc[:, i * P:(i + 1) * P], XT[:, i, :], vb[:, 0, (h0 + i) * P:(h0 + i + 1) * P],
                               start=True, stop=True)
            mm.then_inc(tick(psum_full), 1)
            pe.wait_ge(u_out, 2 * s + 1)
            acc = take_unit(pe, f"r{l}{half}")
            for i in range(HALF):
                mm = pe.matmul(acc[:, i * P:(i + 1) * P], AT[:, i, P:T], U1[:, i * P:(i + 1) * P], start=True, stop=True)
            mm.then_inc(tick(psum_full), 1)
            pe.wait_ge(r_out, s + 1)
            acc = take_unit(pe, f"u2{l}{half}")
            for i in range(HALF):
                mm = pe.matmul(acc[:, i * P:(i + 1) * P], XT[:, HALF + i, :], vb[:, 1, (h0 + i) * P:(h0 + i + 1) * P],
                               start=True, stop=True)
            mm.then_inc(tick(psum_full), 1)
            pe.wait_ge(u_out, 2 * s + 2)
            acc = take_unit(pe, f"o{l}{half}")
            for i in range(HALF):
                c = slice(i * P, (i + 1) * P)
                c2 = slice(512 + i * P, 512 + (i + 1) * P)
                pe.matmul(acc[:, c], QK[:, i, 0:P], U1[:, c], start=True, stop=True)
                pe.matmul(acc[:, c2], QK[:, i, P:T], U1[:, c], start=True, stop=False)
                mm = pe.matmul(acc[:, c2], QK[:, i, T:384], U2[:, c], start=False, stop=True)
            mm.then_inc(tick(psum_full), 1)

        def mixer_act(act, l):
            norm_act(act, f"mix{l}", col(f"norm_mix{l}"))
            for j in range(2):
                rope_act(act, 2 * l + j, f"rqk{l}{j}")
            for j in range(2):
                unit = f"rv{l}{j}"
                i_ = act.activation(v_ret[:, :, j * 512:(j + 1) * 512], full(act, unit)[:, :].rearrange("p (t c) -> p t c", t=TT), ACT.Copy)
                i_.then_inc(tick(ret_v), 1)
                free(unit)
            for j in range(2):
                unit = f"rg{l}{j}"
                i_ = act.activation(o_ret[:, :, j * 512:(j + 1) * 512], full(act, unit)[:, :].rearrange("p (t c) -> p t c", t=TT), ACT.Silu)
                i_.then_inc(tick(ret_g), 1)
                free(unit)
            for j in range(6):
                unit = f"gqkv{l}{j}"
                n = 6 * l + j
                if j >= 3:
                    root_act(act, l, j - 3)
                acc = full(act, unit)
                if j == 0:
                    act.wait_ge(rope_out, 2 * l + 2)
                if j >= 2:
                    act.wait_ge(conv_acc, n - 1)
                    act.wait_ge(conv_out, n - 1)
                act.activation(cin[j % 2][:, :, 3:259], acc[:, :].rearrange("p (a t) -> p a t", a=4), ACT.Copy).then_inc(tick(conv_in), 1)
                w = col(f"conv{l}")
                for a in range(4):
                    i_ = act.activation(cacc[j % 2][:, a, :], acc[:, a * T:(a + 1) * T], ACT.Copy,
                                        scale=w[:, (4 * j + a) * 4 + 3:(4 * j + a) * 4 + 4])
                i_.then_inc(tick(conv_in), 1)
                free(unit)
                if j >= 1:
                    conv_silu(act, l, j - 1)
                if 1 <= j <= 4:
                    square_act(act, l, j - 1)
            root_act(act, l, 3)
            conv_silu(act, l, 5)
            act.activation(nea, col(f"alog{l}"), ACT.Exp).then_inc(tick(ab_abs), 1)
            act.wait_ge(ab_x, l + 1)
            astep(act, act.activation(gab, gx, ACT.Abs))
            astep(act, act.activation(gab2, gab, ACT.Exp, scale=-1.0))
            act.activation(gab, gab2, ACT.Ln, bias=1.0).then_inc(tick(ab_soft), 1)
            acc = full(act, f"ab{l}")
            act.activation(gbeta[:, :, 2:4], acc[:, 0:32].rearrange("p (t c) -> p c t", t=TT)[:, 8:16, :], ACT.Sigmoid).then_inc(tick(ab_soft), 1)
            for j in range(2):
                unit = f"gz{l}{j}"
                i_ = act.activation(o_gdn[:, :, j * 512:(j + 1) * 512], full(act, unit)[:, :].rearrange("p (t c) -> p t c", t=TT), ACT.Silu)
                i_.then_inc(tick(gz_out), 1)
                free(unit)
            turn_act(act, f"oret{l}", oT, col(f"ret_gn{l}"))
            for half in range(2):
                s = 2 * l + half
                for n in range(half * HALF, half * HALF + HALF):
                    i = l * GH + n
                    act.wait_ge(dec_arg, i + 1)
                    act.activation(dec[n % 2], dec[n % 2], ACT.Exp).then_inc(tick(dec_exp), 1)
                if half == 0:
                    merge_gate_act(act, l, "ret", 0)
                for lev in range(1, 7):
                    unit = f"m{lev}{l}{half}"
                    i_ = act.activation(MS.rearrange("p n c -> p (n c)"), full(act, unit)[:, :], ACT.Copy)
                    i_.then_inc(tick(m_out), 1)
                    free(unit)
                    if half == 1 and lev == 2:
                        merge_gate_act(act, l, "gdn", 0)
                merge_gate_act(act, l, ("ret", "gdn")[half], 1)
                for j, u in enumerate((U1, U2)):
                    unit = f"u{j + 1}{l}{half}"
                    i_ = act.activation(u, full(act, unit)[:, 0:512], ACT.Copy)
                    i_.then_inc(tick(u_out), 1)
                    free(unit)
                act.activation(hsqr, full(act, f"o{l}{half}")[:, :], ACT.Square).then_inc(tick(hn_sq), 1)
            turn_act(act, f"ogdn{l}", oT, col(f"gdn_gn{l}"), same=True)

        def merge_gate_act(act, l, br, j):
            unit = f"mg{br}{l}{j}"
            acc = full(act, unit)
            if br == "ret" and j == 1:
                act.wait_ge(merged_out, 4 * l + 1)
            act.activation(sg[2 * (br == "gdn") + j], acc[:, :], ACT.Sigmoid).then_inc(tick(sig_out), 1)
            free(unit)

        def conv_silu(act, l, j):
            act.wait_ge(conv_acc, 6 * l + j + 1)
            act.activation(cv[:, 4 * j:4 * j + 4, :], cacc[j % 2], ACT.Silu).then_inc(tick(conv_out), 1)

        def square_act(act, l, j):
            act.wait_ge(conv_out, 6 * l + j + 1)
            if j >= 2:
                act.wait_ge(*full_at[f"nrm{l}{j - 2}"])
            act.activation(sq[j % 2], cv[:, 4 * j:4 * j + 4, :].rearrange("p a t -> p (a t)"), ACT.Square).then_inc(tick(sq_out), 1)

        def root_act(act, l, j):
            unit = f"nrm{l}{j}"
            acc = full(act, unit)
            if 4 * l + j >= 1:
                act.wait_ge(qk_norm, 4 * l + j)
            i_ = act.activation(root, acc[:, :], ACT.Ln, bias=eps)
            astep(act, i_)
            free(unit)
            act.activation(root, root, ACT.Exp, scale=-0.5).then_inc(tick(nrm_root), 1)

        def mixer_dve(dve, l):
            norm_dve(dve, f"mix{l}", col(f"norm_mix{l}"))
            for j in range(2):
                rope_dve(dve, 2 * l + j, f"rope{l}{j}", qk_ret[:, j * 1024:(j + 1) * 1024], col("sin1"))
            for what in RET_ORDER:
                n = int(what[1])
                unit = f"ret{what}{l}"
                acc = full(dve, unit)
                if what[0] == "s":
                    i_ = dve.tensor_tensor(s_ret[n % 2], acc[:, 0:384], col(f"ret{n}"), ALU.mult)
                    i_.then_inc(tick(ret_s), 1)
                    free(unit)
                    continue
                for t in range(TT):
                    i_ = dve.bn_stats(bst[:, 6 * t:6 * t + 6], acc[:, t * 256:(t + 1) * 256])
                dstep(dve, i_)
                for t in range(TT):
                    i_ = dve.bn_aggr(bag[:, 2 * t:2 * t + 2], bst[:, 6 * t:6 * t + 6])
                dstep(dve, i_)
                for t in range(TT):
                    i_ = dve.tensor_scalar(brs[:, t:t + 1], bag[:, 2 * t + 1:2 * t + 2], EPS, None, ALU.add)
                i_.then_inc(tick(ret_var), 1)
                dve.wait_ge(ret_rs, 4 * l + n + 1)
                for t in range(TT):
                    i_ = dve.tensor_scalar(o_tmp[:, t * 256:(t + 1) * 256], acc[:, t * 256:(t + 1) * 256],
                                           bag[:, 2 * t:2 * t + 1], brs[:, t:t + 1], ALU.subtract, ALU.mult)
                dstep(dve, i_)
                free(unit)
                if n == 0:
                    dve.wait_ge(ret_g, 2 * l + 2)
                o = o_ret[:, :, n * 256:(n + 1) * 256]
                i_ = dve.tensor_tensor(o, o, o_tmp.rearrange("p (t c) -> p t c", t=TT), ALU.mult)
                dstep(dve, i_)
                if n == RET_H - 1:
                    dve.nop().then_inc(tick(nat_ready), 1)
            for k in range(2):
                i_ = dve.memset(cin[k][:, :, 0:3], 0.0)
            dstep(dve, i_)
            def unit_norm(j):
                dve.wait_ge(nrm_root, 4 * l + j + 1)
                x = cv[:, 4 * j:4 * j + 4, :].rearrange("p a t -> p (a t)")
                dve.scalar_tensor_tensor(x, root, P ** -0.5 if j < 2 else 1.0, x, ALU.mult, ALU.mult).then_inc(tick(qk_norm), 1)

            for j in range(6):
                n = 6 * l + j
                if j >= 3:
                    unit_norm(j - 3)
                dve.wait_ge(conv_in, 2 * n + 2)
                w = col(f"conv{l}")
                for tap in (2, 1, 0):
                    for a in range(4):
                        c = (4 * j + a) * 4 + tap
                        i_ = dve.scalar_tensor_tensor(cacc[j % 2][:, a, :], cin[j % 2][:, a, tap:tap + T], w[:, c:c + 1],
                                                      cacc[j % 2][:, a, :], ALU.mult, ALU.add)
                    if tap:
                        dstep(dve, i_)
                i_.then_inc(tick(conv_acc), 1)
            unit_norm(3)
            acc = full(dve, f"ab{l}")
            ga = acc[:, 0:32].rearrange("p (t c) -> p t c", t=TT)[:, :, 0:8]
            g2 = lambda a: a.rearrange("p (t c) -> p t c", t=TT)
            dve.tensor_tensor(g2(gx), ga, col(f"dtb{l}").unsqueeze(1).broadcast_to([P, TT, GH]), ALU.add).then_inc(tick(ab_x), 1)
            dve.wait_ge(ab_x, l + 1)
            dve.wait_ge(ab_abs, l + 1)
            dve.wait_ge(ab_soft, 2 * l + 2)
            i_ = dve.scalar_tensor_tensor(gx, gx, 0.0, gab, ALU.max, ALU.add)
            dstep(dve, i_)
            free(f"ab{l}")
            i_ = dve.scalar_tensor_tensor(gbeta[:, :, 0:2].rearrange("p c t -> p t c"), g2(gx), -1.0,
                                     nea.unsqueeze(1).broadcast_to([P, TT, GH]), ALU.mult, ALU.mult)
            i_.then_inc(tick(g_ready), 1)
            dve.wait_ge(g_ready, l + 1)
            for t in range(TT):
                unit = f"v{l}{t}"
                acc = full(dve, unit)
                i_ = dve.tensor_tensor(vb[:, t, :].rearrange("p (n c) -> p n c", c=P), acc[:, :].rearrange("p (n c) -> p n c", c=P),
                                       gbeta[:, :, 2 + t].unsqueeze(2).broadcast_to([P, GH, P]), ALU.mult)
                i_.then_inc(tick(v_beta), 1)
                free(unit)
            unit = f"gc{l}"
            i_ = dve.tensor_copy(gcn, full(dve, unit)[:, 0:16])
            dstep(dve, i_)
            free(unit)
            turn_dve(dve, f"oret{l}", oT, col(f"ret_gn{l}"))
            for half in range(2):
                solve_dve(dve, l, half)
            turn_dve(dve, f"ogdn{l}", oT, col(f"gdn_gn{l}"), same=True)
            for j in range(2):
                merge_dve(dve, l, "gdn", j)
            add_h(dve, [f"wo{l}{j}" for j in range(2)])

        def merge_dve(dve, l, br, j):
            unit = f"br{br}{l}{j}"
            i = 4 * l + 2 * (br == "gdn") + j
            acc = full(dve, unit)
            dve.wait_ge(sig_out, i + 1)
            if i:
                dve.wait_ge(merged_out, i)
            m = merged[:, 4 * j:4 * j + 4, :].rearrange("p k t -> p (k t)")
            gate = sg[2 * (br == "gdn") + j]
            if br == "ret":
                dve.tensor_tensor(m, acc[:, :], gate, ALU.mult).then_inc(tick(merged_out), 1)
                free(unit)
            else:
                dstep(dve, dve.tensor_tensor(btmp, acc[:, :], gate, ALU.mult))
                free(unit)
                dve.tensor_tensor(m, m, btmp, ALU.add).then_inc(tick(merged_out), 1)

        def add_h(dve, units):
            for j, unit in enumerate(units):
                acc = full(dve, unit)
                hh = h[:, :, j * 512:(j + 1) * 512]
                i_ = dve.tensor_tensor(hh, hh, acc[:, :].rearrange("p (t c) -> p t c", t=TT), ALU.add)
                i_.then_inc(tick(psum_read if j == 0 else h_new), 1)
                free(unit)

        def solve_dve(dve, l, half):
            s = 2 * l + half
            h0 = half * HALF

            def decay(n):
                unit = f"sp{l}{n}"
                acc = full(dve, unit)
                d = dec[n % 2]
                dve.tensor_scalar(d[:, 0:T], acc[:, 0:T], gcn[:, n:n + 1], 0.0, ALU.subtract, ALU.min)
                dve.tensor_scalar(d[:, T:384], acc[:, P:T], gcn[:, GH + n:GH + n + 1], 0.0, ALU.subtract, ALU.min).then_inc(tick(dec_arg), 1)
                dve.tensor_tensor(kb[n % 2], cv[:, 8 + n, :], acc[:, 512:768], ALU.mult).then_inc(tick(kb_out), 1)
                free(unit)

            decay(h0)
            for n in range(h0, h0 + HALF):
                if n + 1 < h0 + HALF:
                    decay(n + 1)
                unit = f"gr{l}{n}"
                acc = full(dve, unit)
                dve.wait_ge(dec_mask, 2 * (l * GH + n) + 2)
                dve.tensor_tensor(AT[:, n - h0, :], acc[:, 0:384], decS[n % 2], ALU.mult).then_inc(tick(a_out), 1)
                dve.tensor_tensor(QK[:, n - h0, :], acc[:, 512:896], decI[n % 2], ALU.mult).then_inc(tick(a_out), 1)
                free(unit)
            if half == 1:
                merge_dve(dve, l, "ret", 1)
            dve.wait_ge(c_out, 7 * s + 1)
            idb = ident.unsqueeze(1).broadcast_to([P, 8, P])
            dve.tensor_tensor(XT, idb, CT, ALU.subtract).then_inc(tick(x_out), 1)
            unit = f"x0{l}{half}"
            i_ = dve.tensor_copy(X.rearrange("p n c -> p (n c)"), full(dve, unit)[:, :])
            i_.then_inc(tick(x_out), 1)
            free(unit)
            xf, xtf = X.rearrange("p n c -> p (n c)"), XT.rearrange("p n c -> p (n c)")
            for lev in range(1, 7):
                if lev < 6:
                    unit = f"p{lev}{l}{half}"
                    acc = full(dve, unit)
                    i_ = dve.tensor_tensor(xf, xf, acc[:, :], ALU.subtract)
                    i_.then_inc(tick(x_out), 1)
                    free(unit)
                unit = f"q{lev}{l}{half}"
                acc = full(dve, unit)
                i_ = dve.tensor_tensor(xtf, xtf, acc[:, :], ALU.subtract)
                i_.then_inc(tick(x_out), 1)
                free(unit)
                if half == 0 and lev == 2:
                    merge_dve(dve, l, "ret", 0)
            unit = f"r{l}{half}"
            acc = full(dve, unit)
            v = vb[:, 1, half * 512:(half + 1) * 512]
            i_ = dve.tensor_tensor(v, v, acc[:, 0:512], ALU.subtract)
            i_.then_inc(tick(r_out), 1)
            free(unit)
            o = o_gdn[:, :, half * 512:(half + 1) * 512].rearrange("p t (n c) -> p t n c", c=P)
            if half == 0:
                dve.wait_ge(gz_out, 2 * l + 2)
            head_norm_dve(dve, s, f"o{l}{half}", o, hsqr)
            if half == 1:
                dve.nop().then_inc(tick(nat_ready), 1)

        def head_norm_dve(dve, n, unit, gated, hsqr):
            dve.wait_ge(hn_sq, n + 1)
            dstep(dve, dve.tensor_reduce(hsum[:, 0:8], hsqr.rearrange("p (n c) -> p n c", c=P), AX, ALU.add))
            dve.tensor_scalar(hms[:, 0:8], hsum[:, 0:8], 1.0 / P, EPS, ALU.mult, ALU.add).then_inc(tick(hn_ms), 1)
            dve.wait_ge(hn_rs, n + 1)
            acc = full(dve, unit)
            i_ = dve.tensor_tensor(hsqr.rearrange("p (n c) -> p n c", c=P), acc[:, :].rearrange("p (n c) -> p n c", c=P),
                                   hrs[:, 0:8].unsqueeze(2).broadcast_to([P, 8, P]), ALU.mult)
            dstep(dve, i_)
            free(unit)
            src = hsqr.rearrange("p (t n c) -> p t n c", n=4, c=P) if len(gated.shape) == 4 else hsqr.rearrange("p (n c) -> p n c", c=P)
            dstep(dve, dve.tensor_tensor(gated, gated, src, ALU.mult))

        def head_norm_pool(pool, n):
            pool.wait_ge(hn_ms, n + 1)
            pool.tensor_tensor(hrs[:, 0:8], hms[:, 0:8], mhalf[:, 0:8], ALU.pow).then_inc(tick(hn_rs), 1)

        def mixer_pool(pool, l):
            stat_pool(pool, f"mix{l}")
            for j in range(2):
                rope_pool(pool, 2 * l + j, qk_ret[:, j * 1024:(j + 1) * 1024], col("cos1"))
            for n in range(RET_H):
                pool.wait_ge(ret_var, 4 * l + n + 1)
                pool.tensor_tensor(brs, brs, mhalf[:, 0:2], ALU.pow).then_inc(tick(ret_rs), 1)
            pool.wait_ge(g_ready, l + 1)
            for half in range(2):
                s = 2 * l + half
                h0 = half * HALF

                def spread(n):
                    if l * GH + n >= 2:
                        pool.wait_ge(kb_out, l * GH + n - 1)
                    pool.tensor_copy(bc[n % 2], gbeta[:, n, :].unsqueeze(2).broadcast_to([P, 4, P])).then_inc(tick(ab_bc), 1)

                spread(h0)
                for n in range(h0, h0 + HALF):
                    i = l * GH + n
                    if n + 1 < h0 + HALF:
                        spread(n + 1)
                    pool.wait_ge(dec_exp, i + 1)
                    if i >= 2:
                        pool.wait_ge(a_out, 2 * (i - 1))
                    pool.tensor_tensor(decI[n % 2], dec[n % 2], col("mI"), ALU.mult).then_inc(tick(dec_mask), 1)
                    pool.tensor_tensor(decS[n % 2], dec[n % 2], col("mS"), ALU.mult).then_inc(tick(dec_mask), 1)
                pool.wait_ge(a_out, 2 * (l * GH + h0 + HALF))
                for lev in range(7):
                    if lev == 1:
                        pool.wait_ge(x_out, 13 * s + 1)
                    if lev >= 2:
                        pool.wait_ge(m_out, 6 * s + lev - 1)
                    m = col(f"mg{lev}").unsqueeze(1).broadcast_to([P, HALF, P])
                    pool.tensor_tensor(CT[:, 0:HALF, :], AT[:, :, 0:P], m, ALU.mult)
                    pool.tensor_tensor(CT[:, HALF:8, :], AT[:, :, T:384], m, ALU.mult).then_inc(tick(c_out), 1)
                head_norm_pool(pool, s)

        sil = area(16, 1024)
        raw = area(17, 1024)
        hid = [area(k, 1024).rearrange("p (a t) -> p a t", a=4) for k in range(3)]
        gateb = area(4, EXPERTS * T).rearrange("p (e t) -> p e t", t=T)
        gbc = area(12, 16 * P).rearrange("p (n c) -> p n c", c=P)
        FFNS = [("ffn0", DENSE_E), ("ffn1", EXPERTS), ("sffn0", DENSE_E), ("sffn1", DENSE_E)]
        ADA_C = 6 * D // EXPERTS
        ADA_E = DEPTH * KT // 2
        ADA_FREE = 4
        ada_slab = [area(6 + 1.5 * k, 2 * ADA_C).rearrange("p (k c) -> p k c", c=ADA_C) for k in range(2)]
        ADA_AFTER = ((0, 1, 2), (3, 4, 5), (6, 7))
        ada_part = [area(9, 6 * D), area(18, 6 * D)]
        GROUP0 = {}
        for name_, e_ in FFNS:
            GROUP0[name_] = sum(3 * e for n, e in FFNS[:FFNS.index((name_, e_))])
        GATE_END, UP_END = (2, 6, 12), (4, 8, 14)
        ffn_at = {}

        def repeat_ticks(before, e_count):
            for k_, v_ in ticks.items():
                ticks[k_] = before.get(k_, 0) + e_count * (v_ - before.get(k_, 0))

        def ffn_pe(pe, name):
            e_count = dict(FFNS)[name]
            g0 = GROUP0[name]
            which = [n for n, _ in FFNS].index(name)
            norm_pe(pe, name)
            if name == "ffn1":
                acc = take_unit(pe, "router")
                wr = col("router").rearrange("p (k c) -> p k c", c=EXPERTS)
                for t in range(TT):
                    for k in range(KT):
                        mm = pe.matmul(acc[:, t * 8:(t + 1) * 8], uT[:, k, t * P:(t + 1) * P], wr[:, k, :],
                                       start=(k == 0), stop=(k == KT - 1))
                mm.then_inc(tick(psum_full), 1)
                pe.wait_ge(gate_b, 1)
                for q in range(2):
                    acc = take_unit(pe, f"gate{q}")
                    for e in range(4):
                        for t in range(TT):
                            mm = pe.matmul(acc[:, e * T + t * P:e * T + (t + 1) * P], gbc[:, t * EXPERTS + 4 * q + e, :],
                                           ident, start=True, stop=True)
                    mm.then_inc(tick(psum_full), 1)
            bank = [take_unit(pe, f"{name}{w}") for w in ("gate", "up", "y0", "y1")]
            n0 = slab_n[0] + extra[0]
            ffn_at[name] = (n0, bank)
            assert slabs[slab_n[0]][0] == name
            pe.wait_ge(y_zero, which + 1)
            before = dict(ticks)
            with pe.Fori(0, e_count) as e:
                j = [0]

                def slab(w, k):
                    m = n0 + j[0]
                    pe.wait_ge(slab_in[m % R], 16 * (m // R + 1) + e * (16 * (PER_E // R)))
                    j[0] += 1
                    return ring[:, m % R, 0:k * w].rearrange("p (k c) -> p k c", c=w)

                def up(g, acc):
                    tiles = GROUPS[g]
                    for half in range(2):
                        w = slab(tiles * P, 4)
                        for m in range(tiles):
                            for k in range(4):
                                mm = pe.matmul(acc[:, m * T:(m + 1) * T], w[:, k, m * P:(m + 1) * P],
                                               uT[:, half * 4 + k, :], start=(half == 0 and k == 0 and m % 2 == 0),
                                               stop=(half == 1 and k == 3), skip_group_check=True)
                        mm.then_inc(tick(slab_used), 1)

                def both(g):
                    pe.wait_ge(silu_out, e * 3 + (g0 + g + 1))
                    up(g, bank[0])
                    pe.wait_ge(hid_out, e * 3 + (g0 + g + 1))
                    up(g, bank[1])

                def down(g):
                    pe.wait_ge(hid_out, e * 3 + (g0 + g + 2))
                    for t0 in range(0, GROUPS[g], 2):
                        k_n = min(2, GROUPS[g] - t0)
                        w = slab(D, k_n)
                        for k in range(k_n):
                            for t in range(TT):
                                for c in range(2):
                                    mm = pe.matmul(bank[2 + t][:, c * 512:(c + 1) * 512], hid[g][:, t0 + k, t * P:(t + 1) * P],
                                                   w[:, k, c * 512:(c + 1) * 512], start=False, stop=True, skip_group_check=True)
                        mm.then_inc(tick(slab_used), 1)

                both(0)
                both(1)
                down(0)
                both(2)
                down(1)
                down(2)
            repeat_ticks(before, e_count)
            slab_n[0] += 1
            extra[0] += PER_E * e_count - 1
            for w in ("y0", "y1"):
                full_at[f"{name}{w}"] = (slab_used, ticks[id(slab_used)])

        def ffn_act(act, name, gain, shift=None):
            e_count, g0 = dict(FFNS)[name], GROUP0[name]
            norm_act(act, name, gain, shift)
            if name == "ffn1":
                act.wait_ge(rt_nm, 1)
                for t in range(TT):
                    c = slice(t * 8, t * 8 + 8)
                    i_ = act.activation(e8[:, c], lg8[:, c], ACT.Exp, bias=nm1[:, t:t + 1])
                i_.then_inc(tick(rt_e), 1)
                for q in range(2):
                    unit = f"gate{q}"
                    i_ = act.activation(gateb[:, 4 * q:4 * q + 4, :].rearrange("p e t -> p (e t)"), full(act, unit)[:, :], ACT.Copy)
                    i_.then_inc(tick(gate_row), 1)
                    free(unit)
            n0, bank = ffn_at[name]
            before = dict(ticks)
            with act.Fori(0, e_count) as e:
                for g in range(3):
                    act.wait_ge(slab_used, e * PER_E + (n0 + GATE_END[g]))
                    act.wait_ge(hid_out, e * 3 + (g0 + g + 1))
                    n = GROUPS[g] * T
                    act.activation(sil[:, 0:n], bank[0][:, 0:n], ACT.Silu).then_inc(tick(silu_out), 1)
            repeat_ticks(before, e_count)
            last[0] = (silu_out, ticks[id(silu_out)])
            free(f"{name}gate")

        def ffn_dve(dve, name, gain, shift=None):
            e_count, g0 = dict(FFNS)[name], GROUP0[name]
            norm_dve(dve, name, gain, shift)
            if name == "ffn1":
                router_dve(dve)
            n0, bank = ffn_at[name]
            for w in range(2):
                before = pair_before[f"{name}y{w}"]
                if before in freed:
                    dve.wait_ge(by_name[freed[before][0]], freed[before][1])
                i_ = dve.memset(bank[2 + w][:, :], 0.0)
            i_.then_inc(tick(y_zero), 1)
            if name == "ffn1":
                dve.wait_ge(gate_row, 2)
                dve.wait_ge(cond_out, 1)
                dve.nop().then_inc(tick(ada_sum, ADA_FREE), ADA_FREE)
            before = dict(ticks)
            with dve.Fori(0, e_count) as e:
                for g in range(3):
                    n = GROUPS[g] * T
                    dve.wait_ge(silu_out, e * 3 + (g0 + g + 2))
                    dve.wait_ge(slab_used, e * PER_E + (n0 + UP_END[g]))
                    hg = hid[g][:, 0:GROUPS[g], :]
                    if name == "ffn1":
                        dve.tensor_tensor(raw[:, 0:n], sil[:, 0:n], bank[1][:, 0:n], ALU.mult).then_inc(tick(hid_raw), 1)
                        dve.wait_ge(hid_raw, e * 3 + (g + 1))
                        dve.tensor_tensor(hg, raw[:, 0:n].rearrange("p (a t) -> p a t", t=T),
                                          gateb[:, bass.ds(e, 1), :].broadcast_to([P, GROUPS[g], T]), ALU.mult).then_inc(tick(hid_out), 1)
                        for i in ADA_AFTER[g]:
                            ada_sum_dve(dve, e, i)
                    else:
                        dve.tensor_tensor(hg.rearrange("p a t -> p (a t)"), sil[:, 0:n], bank[1][:, 0:n], ALU.mult).then_inc(tick(hid_out), 1)
            repeat_ticks(before, e_count)
            last[0] = (hid_out, ticks[id(hid_out)])
            free(f"{name}up")
            if name[0] == "s":
                return
            for t in range(TT):
                acc = full(dve, f"{name}y{t}")
                i_ = dve.tensor_tensor(h[:, t, :], h[:, t, :], acc[:, :], ALU.add)
                i_.then_inc(tick(h_new if t else psum_read), 1)
                free(f"{name}y{t}")

        def router_dve(dve):
            i_ = dve.tensor_copy(lg8, full(dve, "router")[:, 0:16])
            dstep(dve, i_)
            free("router")
            l2 = lg8.rearrange("p (t e) -> p t e", t=TT)
            dve.tensor_reduce(nm1, l2, AX, ALU.max, negate=True).then_inc(tick(rt_nm), 1)
            dstep(dve, dve.memset(sel8, 0.0))
            for j in range(EXPERTS):
                for t in range(TT):
                    b = t * EXPERTS
                    for lo, hi, op in ((0, j, ALU.is_lt), (j + 1, EXPERTS, ALU.is_le)):
                        if hi > lo:
                            s_ = slice(b + lo, b + hi)
                            i_ = dve.scalar_tensor_tensor(sel8[:, s_], lg8[:, s_], lg8[:, b + j:b + j + 1], sel8[:, s_], op, ALU.add)
                dstep(dve, i_)
            dstep(dve, dve.tensor_scalar(sel8, sel8, 1.5, None, ALU.is_lt))
            dve.wait_ge(rt_e, 1)
            dstep(dve, dve.tensor_tensor(e8, e8, sel8, ALU.mult))
            dstep(dve, dve.tensor_reduce(es, e8.rearrange("p (t e) -> p t e", t=TT), AX, ALU.add))
            dstep(dve, dve.reciprocal(es, es))
            for t in range(TT):
                c = slice(t * 8, t * 8 + 8)
                i_ = dve.tensor_scalar(gates[:, c], e8[:, c], es[:, t:t + 1], None, ALU.mult)
            i_.then_inc(tick(rt_l), 1)

        def ffn_pool(pool, name):
            stat_pool(pool, name)
            if name == "ffn1":
                pool.wait_ge(rt_l, 1)
                pool.tensor_copy(gbc, gates.unsqueeze(2).broadcast_to([P, 16, P])).then_inc(tick(gate_b), 1)

        plb = area(0, 2048)
        plt = area(2, 1024)
        plg = [area(16 + k, 1024) for k in range(2)]

        def ple_pe(pe, l):
            w = take_slab(pe, f"ple{l}")
            pT = col(f"pT{l}").rearrange("p (k t) -> p k t", t=T)
            for j in range(2):
                acc = take_unit(pe, f"ple{l}{j}")
                for t in range(TT):
                    for k in range(2):
                        mm = pe.matmul(acc[:, t * 512:(t + 1) * 512], pT[:, k, t * P:(t + 1) * P],
                                       w[:, k, j * 512:(j + 1) * 512], start=(k == 0), stop=(k == 1))
                mm.then_inc(tick(slab_used if j else psum_full), 1)
                filled(f"ple{l}{j}")
            if l == DEPTH - 1:
                ada_pe(pe)
            norm_pe(pe, f"ple{l}")
            for j in range(2):
                linear_n(pe, f"plg{l}", f"plg{l}{j}")

        def ple_act(act, l):
            for j in range(2):
                unit = f"ple{l}{j}"
                i_ = act.activation(plb[:, j * 1024:(j + 1) * 1024], full(act, unit)[:, :], ACT.Copy)
                i_.then_inc(tick(ple_out), 1)
                free(unit)
            norm_act(act, f"ple{l}", col(f"norm_ple{l}"))
            for j in range(2):
                unit = f"plg{l}{j}"
                i_ = act.activation(plg[j], full(act, unit)[:, :], ACT.Sigmoid)
                i_.then_inc(tick(plg_out), 1)
                free(unit)

        def ple_dve(dve, l):
            norm_dve(dve, f"ple{l}", col(f"norm_ple{l}"))
            if l == DEPTH - 1:
                ada_bias_dve(dve)
            for j in range(2):
                dve.wait_ge(ple_out, 2 * l + 2)
                dve.wait_ge(plg_out, 2 * l + j + 1)
                dstep(dve, dve.tensor_tensor(plt, plg[j], plb[:, j * 1024:(j + 1) * 1024], ALU.mult))
                hh = h[:, :, j * 512:(j + 1) * 512]
                i_ = dve.tensor_tensor(hh, hh, plt.rearrange("p (t c) -> p t c", t=TT), ALU.add)
                if j:
                    i_.then_inc(tick(h_new), 1)
                else:
                    dstep(dve, i_)

        row_in, row = area(12, 1024), area(14, 1024)

        def row_dve(dve, n, vec):
            for k in range(KT):
                i_ = dve.tensor_scalar(row_in[:, k * P:(k + 1) * P], ident, vec[:, k:k + 1], None, ALU.mult)
            i_.then_inc(tick(row_rhs), 1)

        def row_pe(pe, n):
            pe.wait_ge(row_rhs, n + 1)
            acc = take_unit(pe, f"row{n}")
            for j in range(2):
                mm = pe.matmul(acc[:, j * 512:(j + 1) * 512], ones, row_in[:, j * 512:(j + 1) * 512], start=True, stop=True)
            mm.then_inc(tick(psum_full), 1)

        def row_act(act, n):
            i_ = act.activation(row, full(act, f"row{n}")[:, :], ACT.Copy)
            i_.then_inc(tick(row_out), 1)
            free(f"row{n}")

        def final_act(act):
            act.wait_ge(h_new, H_BEFORE["final"])
            stat_act(act, "final", h)
            row_act(act, 0)

        def final_dve(dve):
            row_dve(dve, 0, col("norm_final"))
            stat_dve(dve, "final")
            dve.wait_ge(row_out, 1)
            for t in range(TT):
                i_ = dve.scalar_tensor_tensor(h[:, t, :], h[:, t, :], rstd[:, t:t + 1], row, ALU.mult, ALU.mult)
            i_.then_inc(tick(h_new), 1)

        def ada_slabs():
            return [(l, a) for a in range(KT // 2) for l in range(DEPTH)]

        def ada_source(e, l, a):
            w = ins["ada_w_2"][l][a * 2 * P:(a + 1) * 2 * P, :].rearrange("(k p) (e c) -> e p k c", p=P, c=ADA_C)
            return w[bass.ds(e, 1)].rearrange("a p k c -> p (a k) c")

        def ada_sum_dve(dve, e, i):
            l, a = ada_slabs()[i]
            dve.wait_ge(ada_in[i % 2], e * (16 * ADA_E // 2) + 16 * (i // 2 + 1))
            part = ada_part[l].rearrange("p (e c) -> p e c", c=ADA_C)[:, bass.ds(e, 1), :]
            for k in range(2):
                w = ada_slab[i % 2][:, k:k + 1, :]
                x = cond[:, 2 * a + k:2 * a + k + 1]
                dve.wait_ge(ada_sum, e * (2 * ADA_E) + (ADA_FREE + 2 * i + k))
                if a == 0 and k == 0:
                    i_ = dve.tensor_scalar(part, w, x, None, ALU.mult)
                else:
                    i_ = dve.scalar_tensor_tensor(part, w, x, part, ALU.mult, ALU.add)
                i_.then_inc(tick(ada_sum), 1)

        def ada_pe(pe):
            pe.wait_ge(ada_sum, ADA_FREE + 2 * ADA_E * EXPERTS)
            acc = take_unit(pe, "ada")
            for l in range(DEPTH):
                for c in range(6 * KT):
                    mm = pe.matmul(acc[:, l * 6 * KT + c:l * 6 * KT + c + 1], ada_part[l][:, c * P:(c + 1) * P],
                                   ones[:, 0:1], start=True, stop=True)
            mm.then_inc(tick(psum_full), 1)

        def ada_bias_dve(dve):
            acc = full(dve, "ada")
            for l in range(DEPTH):
                i_ = dve.tensor_tensor(col(f"adab{l}"), col(f"adab{l}"), acc[:, l * 6 * KT:(l + 1) * 6 * KT], ALU.add)
            dstep(dve, i_)
            free("ada")

        def ada_dve(dve, l):
            dstep(dve, dve.tensor_copy(mod, col(f"adab{l}")))
            for dst, c, g in ((gmix, 8, 0), (grow, 16, 1), (gmix2, 32, 2), (grow2, 40, 3)):
                i_ = dve.scalar_tensor_tensor(dst, mod[:, c:c + 8], 1.0, col(f"ng{l}{g}"), ALU.add, ALU.mult)
            i_.then_inc(tick(mod_out), 1)
            dve.wait_ge(mod_out, l + 1)

        yb = area(0, 2048).rearrange("p (t d) -> p t d", t=TT)

        def post_act(act, name, n, units):
            for j, unit in enumerate(units):
                acc = full(act, unit)
                if unit[0] == "s":
                    i_ = act.activation(yb[:, j, :], acc[:, :], ACT.Copy)
                else:
                    i_ = act.activation(yb[:, :, j * 512:(j + 1) * 512], acc[:, :].rearrange("p (t c) -> p t c", t=TT), ACT.Copy)
                i_.then_inc(tick(y_out), 1)
                free(unit)
            act.wait_ge(y_out, 2 * n)
            stat_act(act, name, yb)
            row_act(act, n)

        def post_dve(dve, name, n, vec):
            row_dve(dve, n, vec)
            stat_dve(dve, name)
            dve.wait_ge(row_out, n + 1)
            for t in range(TT):
                i_ = dve.scalar_tensor_tensor(yb[:, t, :], yb[:, t, :], rstd[:, t:t + 1], row, ALU.mult, ALU.mult)
                dstep(dve, i_)
                i_ = dve.tensor_tensor(h[:, t, :], h[:, t, :], yb[:, t, :], ALU.add)
                if t:
                    i_.then_inc(tick(h_new), 1)

        NC = T // HG_C
        hq = area(0, 2048).rearrange("p (k t) -> p k t", t=T)
        hk = area(2, 2048).rearrange("p (k t) -> p k t", t=T)
        hf = area(4, 2048).rearrange("p (k t) -> p k t", t=T)
        hv = area(6, 2048).rearrange("p (t d) -> p t d", t=TT)
        hg = area(8, 2048).rearrange("p (t d) -> p t d", t=TT)
        ki = area(10, 2048).rearrange("p (k t) -> p k t", t=T)
        ke = area(12, 2048).rearrange("p (k t) -> p k t", t=T)
        hb = area(14, 2048).rearrange("p (k t) -> p k t", t=T)
        kn = area(16, 2048).rearrange("p (t d) -> p t d", t=TT)
        aT = area(18, 2048).rearrange("p (t n c) -> p t n c", t=TT, c=P)
        S = [area(20 + k, 1024).rearrange("p (n c) -> p n c", c=P) for k in range(2)]
        s_tmp = area(22, 1024).rearrange("p (n c) -> p n c", c=P)
        hsq2 = area(23, 1024)
        lasts = small_tile(GH * NC).rearrange("p (n c) -> p n c", c=NC)

        def hgrn_pe(pe):
            norm_pe(pe, "smix0")
            for j in range(2):
                linear_t(pe, "hq", f"hq{j}")
            for j in range(2):
                linear_t(pe, "hf", f"hf{j}")
            for j in range(2):
                linear_n(pe, "hv", f"hv{j}")
            for j in range(2):
                linear_n(pe, "hgt", f"hgt{j}")
            pe.wait_ge(hg_mul, 6)
            for t in range(TT):
                acc = take_unit(pe, f"kn{t}")
                for n in range(GH):
                    mm = pe.transpose(acc[:, n * P:(n + 1) * P], ke[:, n, t * P:(t + 1) * P], ident)
                mm.then_inc(tick(psum_full), 1)
            for t in range(TT):
                acc = take_unit(pe, f"ha{t}")
                for n in range(GH):
                    c = slice(t * P, (t + 1) * P)
                    mm = pe.matmul(acc[:, n * P:(n + 1) * P], ki[:, n, c], hq[:, n, c], start=True, stop=True)
                mm.then_inc(tick(psum_full), 1)
            pe.wait_ge(hg_nat, 2)
            pe.wait_ge(hg_v, 2)

            def grow_state(c):
                t, r = c // 4, HG_C * (c % 4)
                acc_u = take_unit(pe, f"hu{c}")
                for n in range(GH):
                    mm = pe.matmul(acc_u[:, n * P:(n + 1) * P], kn[r:r + HG_C, t, n * P:(n + 1) * P],
                                   hv[r:r + HG_C, t, n * P:(n + 1) * P], start=True, stop=True, tile_position=(r, 0))
                mm.then_inc(tick(psum_full), 1)

            for t in range(TT):
                pe.wait_ge(hg_a, t + 1)
                acc = take_unit(pe, f"ho{t}")
                for n in range(GH):
                    pe.matmul(acc[:, n * P:(n + 1) * P], aT[:, t, n, :], hv[:, t, n * P:(n + 1) * P],
                              start=(n % 4 == 0), stop=True, skip_group_check=True)
                for c in range(4 * t, 4 * t + 4):
                    r = HG_C * (c % 4)
                    if c:
                        pe.wait_ge(hg_s, c)
                        for n in range(GH):
                            mm = pe.matmul(acc[r:r + HG_C, n * P:(n + 1) * P], hq[:, n, c * HG_C:(c + 1) * HG_C],
                                           S[c % 2][:, n, :], start=False, stop=True, skip_group_check=True,
                                           tile_position=(0, r))
                        if c % 4 == 3:
                            current[0] = f"ho{t}"
                            mm.then_inc(tick(psum_full), 1)
                    if c % 4 < 3:
                        grow_state(c)
                    elif c < NC - 1:
                        grow_state(c)
            turn_pe(pe, "so0", hg)
            pe.wait_ge(t_ready_lo, turned("so0"))
            pe.wait_ge(t_ready_hi, turned("so0"))
            for j in range(2):
                linear_n(pe, "ho", f"wo{j}", oT)
            row_pe(pe, 1)

        def hgrn_act(act):
            norm_act(act, "smix0", gmix, mod[:, 0:8])
            flat = lambda x, j: x[:, 4 * j:4 * j + 4, :].rearrange("p a t -> p (a t)")
            for j in range(2):
                unit = f"hq{j}"
                act.activation(flat(hq, j), full(act, unit)[:, :], ACT.Silu).then_inc(tick(hg_q), 1)
                free(unit)
            for j in range(2):
                unit = f"hf{j}"
                acc = full(act, unit)
                act.activation(flat(hf, j), acc[:, :], ACT.Sigmoid).then_inc(tick(hg_f), 1)
                act.activation(flat(hk, j), acc[:, :], ACT.Sigmoid, scale=-1.0).then_inc(tick(hg_f), 1)
                free(unit)
            for j in range(2):
                act.wait_ge(hg_ff, j + 1)
                act.activation(flat(hf, j), flat(hf, j), ACT.Ln).then_inc(tick(hg_ln), 1)
            for j in range(2):
                act.wait_ge(hg_b, 2 * j + 1)
                act.activation(flat(hf, j), flat(hb, j), ACT.Exp).then_inc(tick(hg_exp), 1)
                act.activation(flat(ki, j), flat(hb, j), ACT.Exp, scale=-1.0).then_inc(tick(hg_exp), 1)
                act.wait_ge(hg_b, 2 * j + 2)
                act.activation(flat(ke, j), flat(ke, j), ACT.Exp).then_inc(tick(hg_exp), 1)
            for unit, dst, f_ in (("hv0", hv, ACT.Copy), ("hv1", hv, ACT.Copy), ("hgt0", hg, ACT.Silu), ("hgt1", hg, ACT.Silu)):
                j = int(unit[-1])
                act.activation(dst[:, :, j * 512:(j + 1) * 512], full(act, unit)[:, :].rearrange("p (t c) -> p t c", t=TT), f_).then_inc(tick(hg_v if f_ == ACT.Copy else hg_gt), 1)
                free(unit)
            for t in range(TT):
                act.activation(kn[:, t, :], full(act, f"kn{t}")[:, :], ACT.Copy).then_inc(tick(hg_nat), 1)
                free(f"kn{t}")
            for t in range(TT):
                act_sq = full(act, f"ho{t}")
                if t:
                    act.wait_ge(hn_gated, 1)
                act.activation(hsq2, act_sq[:, :], ACT.Square).then_inc(tick(hn_sq), 1)
            turn_act(act, "so0", oT, col("hgng"))
            post_act(act, "spost0", 1, ["wo0", "wo1"])

        def hgrn_dve(dve):
            norm_dve(dve, "smix0", gmix, mod[:, 0:8])
            dve.wait_ge(hg_lb, 2)
            dstep(dve, dve.reciprocal(lbr, lbe))
            dstep(dve, dve.tensor_tensor(lbr, lbe, lbr, ALU.mult))
            dstep(dve, dve.tensor_tensor(lbs, lbr, lbr, ALU.subtract))
            dstep(dve, dve.tensor_scalar(oml, lbs, -1.0, 1.0, ALU.mult, ALU.add))
            flat = lambda x, j: x[:, 4 * j:4 * j + 4, :].rearrange("p a t -> p (a t)")
            dve.memset(aT.rearrange("p t n c -> p (t n c)"), 0.0)
            for j in range(2):
                dve.wait_ge(hg_f, 2 * j + 2)
                for n in range(4 * j, 4 * j + 4):
                    dve.tensor_scalar(hf[:, n, :], hf[:, n, :], oml[:, n:n + 1], lbs[:, n:n + 1], ALU.mult, ALU.add)
                    i_ = dve.tensor_scalar(hk[:, n, :], hk[:, n, :], oml[:, n:n + 1], None, ALU.mult)
                i_.then_inc(tick(hg_ff), 1)
            for j in range(2):
                dve.wait_ge(hg_ln, j + 1)
                for n in range(4 * j, 4 * j + 4):
                    i_ = dve.tensor_tensor_scan(hb[:, n, :], col("reset"), hf[:, n, :], 0.0, ALU.mult, ALU.add)
                i_.then_inc(tick(hg_b), 1)
                dve.wait_ge(hg_b, 2 * j + 1)
                bj = hb[:, 4 * j:4 * j + 4, :].rearrange("p n (c s) -> p (n c) s", s=HG_C)
                dve.tensor_tensor(ke[:, 4 * j:4 * j + 4, :].rearrange("p n (c s) -> p (n c) s", s=HG_C),
                                  bj[:, :, HG_C - 1:HG_C].broadcast_to([P, 4 * NC, HG_C]), bj, ALU.subtract).then_inc(tick(hg_b), 1)
            for j in range(2):
                dve.wait_ge(hg_exp, 3 * j + 1)
                dve.wait_ge(hg_q, j + 1)
                dve.tensor_copy(lasts[:, 4 * j:4 * j + 4, :], hf[:, 4 * j:4 * j + 4, :].rearrange("p n (c s) -> p n c s", s=HG_C)[:, :, :, HG_C - 1])
                dve.tensor_tensor(flat(hq, j), flat(hq, j), flat(hf, j), ALU.mult).then_inc(tick(hg_mul), 1)
                dve.wait_ge(hg_exp, 3 * j + 2)
                dve.tensor_tensor(flat(ki, j), flat(ki, j), flat(hk, j), ALU.mult).then_inc(tick(hg_mul), 1)
                dve.wait_ge(hg_exp, 3 * j + 3)
                dve.tensor_tensor(flat(ke, j), flat(ke, j), flat(hk, j), ALU.mult).then_inc(tick(hg_mul), 1)
            for t in range(TT):
                unit = f"ha{t}"
                acc = full(dve, unit)
                m = col("hg").bitcast(U32).unsqueeze(1).broadcast_to([P, GH, P])
                dve.copy_predicated(aT[:, t], m, acc[:, :].rearrange("p (n c) -> p n c", c=P)).then_inc(tick(hg_a), 1)
                free(unit)

            def state(c):
                unit = f"hu{c}"
                acc = full(dve, unit)
                v = acc[:, :].rearrange("p (n c) -> p n c", c=P)
                if c == 0:
                    dve.tensor_copy(S[1], v).then_inc(tick(hg_s), 1)
                    free(unit)
                    dve.wait_ge(hg_s, 1)
                    return
                dstep(dve, dve.tensor_tensor(s_tmp, S[c % 2], lasts[:, :, c:c + 1].broadcast_to([P, GH, P]), ALU.mult))
                dve.tensor_tensor(S[(c + 1) % 2], s_tmp, v, ALU.add).then_inc(tick(hg_s), 1)
                free(unit)
                dve.wait_ge(hg_s, c + 1)

            for t in range(TT):
                for c in range(4 * t, min(4 * t + 4, NC - 1)):
                    if c == 3:
                        head_norm_dve(dve, 4, "ho0", hg[:, 0, :].rearrange("p (n c) -> p n c", c=P), hsq2)
                        dve.nop().then_inc(tick(hn_gated), 1)
                    state(c)
            head_norm_dve(dve, 5, "ho1", hg[:, 1, :].rearrange("p (n c) -> p n c", c=P), hsq2)
            dve.nop().then_inc(tick(nat_ready), 1)
            turn_dve(dve, "so0", oT, col("hgng"))
            post_dve(dve, "spost0", 1, grow)

        PAIRS = GH // 2
        cos2, sin2 = area(24, T), area(24.25, T)
        ang, kf = area(24.5, T), area(24.75, T)
        posi = kf.bitcast(I32)
        aq, ak = ([area(6 * (g % 2) + o, 2048).rearrange("p (k t) -> p k t", t=T) for g in range(3)] for o in (0, 2))
        av = [area(6 * (g % 2) + 4, 2048).rearrange("p (t d) -> p t d", t=TT) for g in range(3)]
        ao = [area(12 + 2 * g, 2048).rearrange("p (t d) -> p t d", t=TT) for g in range(3)]
        xf_ = xn.rearrange("p t d -> p (t d)")
        nmx, zs, lse, rz, wg = (xf_[:, 1536 + 48 * k:1584 + 48 * k] for k in range(5))
        mx3, wsum = (xf_[:, 1792 + 16 * k:1808 + 16 * k] for k in range(2))
        ss = [area(18, 768).rearrange("p (n c) -> p n c", n=2), area(21, 768).rearrange("p (n c) -> p n c", n=2)]
        pt = [xf_[:, 768 * k:768 * (k + 1)].rearrange("p (n c) -> p n c", n=2) for k in range(2)]

        def attention_order():
            lin = []
            for g in range(3):
                chunks = [("lin", g, j) for j in range(6)]
                seq = [chunks[0]]
                for j in range(1, 5):
                    seq += [chunks[j], ("rope", g, j - 1)]
                seq.append(chunks[5])
                lin.append(seq)
            steps_ = [("s", 0), ("s", 1), ("t", 0), ("o", 0), ("s", 2), ("t", 1), ("o", 1), ("s", 3), ("t", 2), ("o", 2), ("t", 3), ("o", 3)]
            seq = list(lin[0])
            for g in range(3):
                nxt = list(lin[g + 1]) if g < 2 else []
                for i, (w, pr) in enumerate(steps_):
                    seq.append((w, g, pr))
                    if nxt:
                        seq.append(nxt.pop(0))
                seq += nxt
            return seq

        AT_SEQ = attention_order()
        ROPE0 = 2 * DEPTH

        def chunk_dst(g, j):
            return (aq, aq, ak, ak)[j][g][:, 4 * (j % 2):4 * (j % 2) + 4, :].rearrange("p a t -> p (a t)")

        def attn_pe(pe):
            norm_pe(pe, "smix1")
            pe.wait_ge(rope_tab, 1)
            for what, g, j in AT_SEQ:
                i = g * PAIRS + j
                if what == "lin":
                    (linear_t if j < 4 else linear_n)(pe, f"at{g}{j // 2}", f"al{g}{j}")
                elif what == "rope":
                    rope_pe(pe, ROPE0 + 4 * g + j, f"ar{g}{j}", col("rot2"))
                elif what == "s":
                    pe.wait_ge(rope_out, ROPE0 + 4 * g + 4)
                    acc = take_unit(pe, f"as{g}{j}")
                    for n in range(2):
                        q, k = aq[g][:, 2 * j + n, :], ak[g][:, 2 * j + n, :]
                        pe.matmul(acc[:, n * 512:n * 512 + P], q[:, 0:P], k[:, 0:P], start=True, stop=True)
                        mm = pe.matmul(acc[:, n * 512 + P:n * 512 + 384], q[:, P:T], k, start=True, stop=True)
                    mm.then_inc(tick(psum_full), 1)
                elif what == "t":
                    pe.wait_ge(at_p, i + 1)
                    acc = take_unit(pe, f"aw{g}{j}")
                    for n in range(2):
                        for b in range(3):
                            mm = pe.transpose(acc[:, n * 512 + b * P:n * 512 + (b + 1) * P], ss[j % 2][:, n, b * P:(b + 1) * P], ident)
                    mm.then_inc(tick(psum_full), 1)
                else:
                    pe.wait_ge(at_t, i + 1)
                    pe.wait_ge(at_v, 2 * g + 2)
                    acc = take_unit(pe, f"ao{g}{j}")
                    for n in range(2):
                        p_ = pt[j % 2][:, n, :]
                        v = av[g][:, :, (2 * j + n) * P:(2 * j + n + 1) * P]
                        c, c2 = slice(n * P, (n + 1) * P), slice(512 + n * P, 512 + (n + 1) * P)
                        pe.matmul(acc[:, c], p_[:, 0:P], v[:, 0, :], start=True, stop=True)
                        pe.matmul(acc[:, c2], p_[:, P:T], v[:, 0, :], start=True, stop=False)
                        mm = pe.matmul(acc[:, c2], p_[:, T:384], v[:, 1, :], start=False, stop=True)
                    mm.then_inc(tick(psum_full), 1)
            turn_pe(pe, "so1", ao[0])
            pe.wait_ge(t_ready_lo, turned("so1"))
            pe.wait_ge(t_ready_hi, turned("so1"))
            for j in range(2):
                linear_n(pe, "ao", f"wao{j}", oT)
            row_pe(pe, 3)

        def attn_act(act):
            norm_act(act, "smix1", gmix, mod[:, 0:8])
            act.dma_start(posi, ins["pos"]).then_inc(pos_in, 16)
            act.wait_ge(at_part, 1)
            act.activation(sin2, sin2, ACT.Sin).then_inc(tick(tab_sin), 1)
            act.activation(cos2, cos2, ACT.Sin).then_inc(tick(rope_tab), 1)
            for what, g, j in AT_SEQ:
                i = g * PAIRS + j
                if what == "lin":
                    if j < 4:
                        rope_act(act, ROPE0 + 4 * g + j, f"al{g}{j}")
                    else:
                        unit = f"al{g}{j}"
                        if g == 2 and j == 4:
                            act.wait_ge(at_o, PAIRS)
                        act.activation(av[g][:, :, (j - 4) * 512:(j - 3) * 512], full(act, unit)[:, :].rearrange("p (t c) -> p t c", t=TT), ACT.Copy).then_inc(tick(at_v), 1)
                        free(unit)
                elif what == "s":
                    act.wait_ge(at_s, i + 1)
                    for n in range(2):
                        for t, (a, b) in enumerate(((0, P), (P, 384))):
                            c = g * 16 + (2 * j + n) * 2 + t
                            i_ = act.activation(ss[j % 2][:, n, a:b], ss[j % 2][:, n, a:b], ACT.Exp, bias=nmx[:, c:c + 1],
                                                accum_out=zs[:, c:c + 1])
                    i_.then_inc(tick(at_p), 1)
                elif what == "t":
                    unit = f"aw{g}{j}"
                    act.activation(pt[j % 2], full(act, unit)[:, :].rearrange("p (n c) -> p n c", n=2)[:, :, 0:384], ACT.Copy).then_inc(tick(at_t), 1)
                    free(unit)
            act.wait_ge(at_p, 3 * PAIRS)
            act.activation(lse, zs, ACT.Ln).then_inc(tick(at_lse), 1)
            act.wait_ge(at_part, 2)
            act.activation(wg, wg, ACT.Exp).then_inc(tick(at_lse), 1)
            turn_act(act, "so1", oT, ones[:, 0:8])
            post_act(act, "spost1", 3, ["wao0", "wao1"])

        C1 = 6.28125
        C2 = 0.00193500518798828125
        C3 = 2 * np.pi - C1 - C2
        PI_IN = 3.1415925

        def attn_dve(dve):
            norm_dve(dve, "smix1", gmix, mod[:, 0:8])
            dve.wait_ge(pos_in, 16)
            dstep(dve, dve.tensor_copy(ang, posi))
            dstep(dve, dve.tensor_scalar(ang, ang, col("freq2"), None, ALU.mult))
            dstep(dve, dve.tensor_scalar(kf, ang, 1.0 / (2 * np.pi), 12582912.0, ALU.mult, ALU.add))
            dstep(dve, dve.tensor_scalar(kf, kf, 12582912.0, None, ALU.subtract))
            for c in (C1, C2, C3):
                dstep(dve, dve.scalar_tensor_tensor(ang, kf, -c, ang, ALU.mult, ALU.add))
            dstep(dve, dve.tensor_scalar(sin2, ang, PI_IN, -PI_IN, ALU.min, ALU.max))
            dstep(dve, dve.tensor_scalar(cos2, sin2, float(np.pi / 2), None, ALU.add))
            dstep(dve, dve.tensor_scalar(kf, cos2, float(np.pi), -2 * np.pi, ALU.is_gt, ALU.mult))
            dstep(dve, dve.tensor_tensor(cos2, cos2, kf, ALU.add))
            dve.tensor_scalar(cos2, cos2, PI_IN, -PI_IN, ALU.min, ALU.max).then_inc(tick(at_part), 1)
            dve.wait_ge(rope_tab, 1)
            w4 = lambda x: x.rearrange("p (n t) -> p t n", t=TT).unsqueeze(3)
            for what, g, j in AT_SEQ:
                if what == "rope":
                    rope_dve(dve, ROPE0 + 4 * g + j, f"ar{g}{j}", chunk_dst(g, j), sin2)
                elif what == "s":
                    unit = f"as{g}{j}"
                    acc = full(dve, unit)
                    if g * PAIRS + j >= 2:
                        dve.wait_ge(at_t, g * PAIRS + j - 1)
                    v = ss[j % 2]
                    m = col(f"at{g}").unsqueeze(1).broadcast_to([P, 2, 384])
                    i_ = dve.scalar_tensor_tensor(v, acc[:, :].rearrange("p (n c) -> p n c", n=2)[:, :, 0:384], P ** -0.5, m, ALU.mult, ALU.add)
                    dstep(dve, i_)
                    free(unit)
                    c = g * 16 + 4 * j
                    nv = nmx[:, c:c + 4].rearrange("p (n t) -> p t n", t=TT)
                    dve.tensor_reduce(nv[:, 0, :], v[:, :, 0:P], AX, ALU.max, negate=True)
                    dve.tensor_reduce(nv[:, 1, :], v[:, :, P:384], AX, ALU.max, negate=True).then_inc(tick(at_s), 1)
                elif what == "o":
                    unit = f"ao{g}{j}"
                    c = g * 16 + 4 * j
                    dve.wait_ge(at_p, g * PAIRS + j + 1)
                    dstep(dve, dve.reciprocal(rz[:, c:c + 4], zs[:, c:c + 4]))
                    acc = full(dve, unit)
                    src = acc[:, :].rearrange("p (t n c) -> p t n c", t=TT, c=P)[:, :, 0:2, :]
                    dst = ao[g][:, :, j * 256:(j + 1) * 256].rearrange("p t (n c) -> p t n c", c=P)
                    dve.tensor_tensor(dst, src, w4(rz[:, c:c + 4]).broadcast_to([P, TT, 2, P]), ALU.mult).then_inc(tick(at_o), 1)
                    free(unit)
            dve.wait_ge(at_lse, 1)
            dstep(dve, dve.tensor_tensor(lse, lse, nmx, ALU.subtract))
            dstep(dve, dve.tensor_tensor(mx3, lse[:, 0:16], lse[:, 16:32], ALU.max))
            dstep(dve, dve.tensor_tensor(mx3, mx3, lse[:, 32:48], ALU.max))
            g3 = lambda x: x.rearrange("p (g n) -> p g n", g=3)
            dve.tensor_tensor(g3(wg), g3(lse), mx3.unsqueeze(1).broadcast_to([P, 3, 16]), ALU.subtract).then_inc(tick(at_part), 1)
            dve.wait_ge(at_lse, 2)
            dstep(dve, dve.tensor_tensor(wsum, wg[:, 0:16], wg[:, 16:32], ALU.add))
            dstep(dve, dve.tensor_tensor(wsum, wsum, wg[:, 32:48], ALU.add))
            dstep(dve, dve.reciprocal(wsum, wsum))
            dstep(dve, dve.tensor_tensor(g3(wg), g3(wg), wsum.unsqueeze(1).broadcast_to([P, 3, 16]), ALU.mult))
            for g in range(3):
                o = ao[g].rearrange("p t (n c) -> p t n c", c=P)
                i_ = dve.tensor_tensor(o, o, w4(wg[:, g * 16:(g + 1) * 16]).broadcast_to([P, TT, GH, P]), ALU.mult)
            dstep(dve, i_)
            dstep(dve, dve.tensor_tensor(ao[0], ao[0], ao[1], ALU.add))
            dve.tensor_tensor(ao[0], ao[0], ao[2], ALU.add).then_inc(tick(nat_ready), 1)
            turn_dve(dve, "so1", oT, ones[:, 0:8])
            dve.wait_ge(*full_at["t1so1"])
            post_dve(dve, "spost1", 3, grow)

        def stages_pe():
            for l in range(DEPTH):
                yield lambda: mixer_pe(pe_[0], l)
                yield lambda: ffn_pe(pe_[0], f"ffn{l}")
                yield lambda: ple_pe(pe_[0], l)
            yield lambda: row_pe(pe_[0], 0)
            for l in range(DEPTH):
                yield lambda: None
                yield lambda: (attn_pe if l % 2 else hgrn_pe)(pe_[0])
                yield lambda: (ffn_pe(pe_[0], f"sffn{l}"), row_pe(pe_[0], 2 + 2 * l))

        def run(gen):
            for stage in gen:
                stage()

        pe_ = [None]

        @block.tensor
        def _(pe):
            pe_[0] = pe
            pe.wait_ge(small_in, 16)
            run(stages_pe())

        @block.scalar
        def _(act):
            def stages():
                for l in range(DEPTH):
                    yield lambda: mixer_act(act, l)
                    yield lambda: ffn_act(act, f"ffn{l}", col(f"norm_ffn{l}"))
                    yield lambda: ple_act(act, l)
                yield lambda: final_act(act)
                for l in range(DEPTH):
                    yield lambda: None
                    yield lambda: (attn_act if l % 2 else hgrn_act)(act)
                    yield lambda: (ffn_act(act, f"sffn{l}", gmix2, mod[:, 24:32]),
                                   post_act(act, f"spostf{l}", 2 + 2 * l, [f"sffn{l}y0", f"sffn{l}y1"]))

            act.dma_start(small[:, :], ins["small"]).then_inc(small_in, 16)
            act.nop().then_inc(tick(silu_out), 1)
            act.wait_ge(small_in, 16)
            act.activation(cond, col("cond"), ACT.Silu).then_inc(tick(cond_out), 1)
            act.wait_ge(hg_lb, 1)
            act.activation(lbe, lbs, ACT.Exp).then_inc(tick(hg_lb), 1)
            run(stages())

        @block.vector
        def _(dve):
            def stages():
                for l in range(DEPTH):
                    yield lambda: mixer_dve(dve, l)
                    yield lambda: ffn_dve(dve, f"ffn{l}", col(f"norm_ffn{l}"))
                    yield lambda: ple_dve(dve, l)
                yield lambda: final_dve(dve)
                for l in range(DEPTH):
                    yield lambda: ada_dve(dve, l)
                    yield lambda: (attn_dve if l % 2 else hgrn_dve)(dve)
                    yield lambda: (ffn_dve(dve, f"sffn{l}", gmix2, mod[:, 24:32]),
                                   post_dve(dve, f"spostf{l}", 2 + 2 * l, grow2))

            dve.nop().then_inc(tick(hid_out), 1)
            dve.wait_ge(small_in, 16)
            dve.wait_ge(x_in, 16)
            dve.tensor_tensor(lbs, col("hglb"), col("hglb"), ALU.subtract).then_inc(tick(hg_lb), 1)
            run(stages())

        @block.gpsimd
        def _(pool):
            def stages():
                for l in range(DEPTH):
                    yield lambda: mixer_pool(pool, l)
                    yield lambda: ffn_pool(pool, f"ffn{l}")
                    yield lambda: stat_pool(pool, f"ple{l}")
                yield lambda: stat_pool(pool, "final")
                for l in range(DEPTH):
                    yield lambda: None
                    if l % 2 == 0:
                        yield lambda: (stat_pool(pool, "smix0"), head_norm_pool(pool, 4), head_norm_pool(pool, 5), stat_pool(pool, "spost0"))
                    else:
                        yield lambda: attn_pool(pool)
                    yield lambda: (stat_pool(pool, f"sffn{l}"), stat_pool(pool, f"spostf{l}"))

            def attn_pool(pool):
                stat_pool(pool, "smix1")
                pool.wait_ge(rope_tab, 1)
                for what, g, j in AT_SEQ:
                    if what == "rope":
                        if g == 2 and j % 2 == 0:
                            pool.wait_ge(at_s, PAIRS)
                        rope_pool(pool, ROPE0 + 4 * g + j, chunk_dst(g, j), cos2)
                stat_pool(pool, "spost1")

            pool.wait_ge(small_in, 16)
            run(stages())

        @block.sync
        def _(sp):
            sp.dma_start(h[:, :, :], ins["x"][0].rearrange("(t p) d -> p t d", p=P)).then_inc(x_in, 16)
            n = 0
            for name, src, kt, c in slabs[:slab_n[0]]:
                if src is not None:
                    if n >= R:
                        sp.wait_ge(slab_used, n - R + 1)
                    dst = ring[:, n % R, 0:kt * c].rearrange("p (k c) -> p k c", c=c)
                    sp.dma_start(dst, src).then_inc(slab_in[n % R], 16)
                    n += 1
                    continue
                gate, up, down = ffn_weights(name)
                with sp.Fori(0, kt) as e:
                    for j, (what, a, b) in enumerate(ffn_slabs()):
                        sp.wait_ge(slab_used, e * PER_E + (n + j - R + 1))
                        slot = (n + j) % R
                        if what == "d":
                            dst = ring[:, slot, 0:b * D].rearrange("p (k c) -> p k c", c=D)
                            src = down(e, a * P, b * P).rearrange("a (k p) c -> p (a k) c", p=P)
                        else:
                            w = GROUPS[a] * P
                            dst = ring[:, slot, 0:4 * w].rearrange("p (k c) -> p k c", c=w)
                            src = (gate if what == "g" else up)(e, b * 512, sum(GROUPS[:a]) * P, w)
                            src = src.rearrange("a (k p) c -> p (a k) c", p=P)
                        sp.dma_start(dst, src).then_inc(slab_in[slot], 16)
                        i = (j - 1) // 2
                        if name == "ffn1" and j % 2 and i < ADA_E:
                            sp.wait_ge(ada_sum, e * (2 * ADA_E) + 2 * i + 2)
                            sp.dma_start(ada_slab[i % 2], ada_source(e, *ada_slabs()[i])).then_inc(ada_in[i % 2], 16)
                n += PER_E * kt
            sp.wait_ge(h_new, len(H_ORDER))
            sp.dma_start(out[0].rearrange("(t p) d -> p t d", p=P), h[:, :, :]).then_inc(out_done, 16)
            sp.wait_ge(out_done, 16)

        unit_freed.clear()
        unit_freed.update(freed_now)


_BIG = ["x", "w_in", "w_br_ret", "w_br_gdn", "w_out", "w_ple", "w_ple_gate", "ffn_w_gate", "ffn_w_up", "ffn_w_down",
        "exp_w_gate", "exp_w_up", "exp_w_down", "ada_w_2", "hgrn_w_in_2", "hgrn_w_out_2", "attn_w_in_2", "attn_w_out_2",
        "ffn_w_in_2", "ffn_w_out_2"]


def layout(inputs):
    x = {k: np.asarray(v) for k, v in inputs.items()}
    blocks = host_layout(x)
    columns, at = {}, 0
    for k, v in blocks.items():
        columns[k] = (at, v.shape[1])
        at += v.shape[1]
    arrays = {k: np.ascontiguousarray(x[k]) for k in _BIG}
    arrays["small"] = np.ascontiguousarray(np.concatenate(list(blocks.values()), 1))
    arrays["pos"] = np.ascontiguousarray(np.broadcast_to(x["positions_2"], (P, T)))
    return arrays, columns


def kernel(**inputs):
    import concourse.bacc as bacc
    from concourse.bass_utils import run_bass_kernel_spmd

    arrays, columns = layout(inputs)

    def write(nc, freed):
        ins = {k: nc.dram_tensor(f"in_{k}", a.shape, mybir.dt.from_np(a.dtype), kind="ExternalInput").ap()
               for k, a in arrays.items()}
        out = nc.dram_tensor("out_h", (1, T, D), F32, kind="ExternalOutput").ap()
        build(nc, columns, ins, out, freed)

    freed = {}
    write(bacc.Bacc("TRN2", target_bir_lowering=False, num_devices=1), freed)
    nc = bacc.Bacc("TRN2", target_bir_lowering=False, num_devices=1)
    write(nc, freed)
    r = run_bass_kernel_spmd(nc, [{f"in_{k}": a for k, a in arrays.items()}], core_ids=[0])
    return r.results[0]["out_h"]
```
